# Optimizing a Trainium2 kernel written in Bass

```python
import jax, jax.numpy as jnp
from jax import lax
import numpy as np
import math

D_MODEL = 1024
BATCH = 1
SEQ = 512
DEPTH = 2

GRID_W = 64
CTX_LEN = 256
A_WIDTH = 512
B_WIDTH = 512
A_CONV = 3
B_CONV = 31
AB_IN = 3 * A_WIDTH + 2 * B_WIDTH
AB_OUT = A_WIDTH + B_WIDTH
N_HEADS = 16
N_KV_HEADS = 4
HEAD_DIM = 64
Q_GROUP = N_HEADS // N_KV_HEADS
Q_W = N_HEADS * HEAD_DIM
KV_W = N_KV_HEADS * HEAD_DIM
WINDOW = 128
BLOCK = 128
ROPE_THETA = 10000.0
D_FF = 2816
FFN_CONV = 3
EPS = 1e-6
NEG_INF = -1e30
N_EVEN = (DEPTH + 1) // 2
N_ODD = DEPTH // 2


def rmsnorm(x, g):
    xf = x.astype(jnp.float32)
    y = xf * lax.rsqrt(jnp.mean(xf * xf, axis=-1, keepdims=True) + EPS)
    return (y * g.astype(jnp.float32)).astype(x.dtype)

def layernorm(x, g, b):
    xf = x.astype(jnp.float32)
    mu = jnp.mean(xf, axis=-1, keepdims=True)
    var = jnp.mean(jnp.square(xf - mu), axis=-1, keepdims=True)
    y = (xf - mu) * lax.rsqrt(var + EPS)
    return (y * g.astype(jnp.float32) + b.astype(jnp.float32)).astype(x.dtype)

def modulate(x, shift, scale):
    return x * (1.0 + scale) + shift

def adaln(cond, w_mod, b_mod):
    m = jax.nn.silu(cond) @ w_mod + b_mod
    return jnp.split(m, 6, axis=-1)

def dwconv(x, w):
    k = w.shape[0]
    return lax.conv_general_dilated(
        x, w[:, None, :], window_strides=(1,), padding=[(k // 2, k // 2)],
        dimension_numbers=('NWC', 'WIO', 'NWC'), feature_group_count=x.shape[-1])

def axial_rope_tables(length):
    rows = length // GRID_W
    row = jnp.repeat(jnp.arange(rows), GRID_W).astype(jnp.float32)
    col = jnp.tile(jnp.arange(GRID_W), rows).astype(jnp.float32)
    n_freq = HEAD_DIM // 4
    inv_freq = ROPE_THETA ** (-jnp.arange(n_freq, dtype=jnp.float32) / n_freq)
    ang = jnp.concatenate([row[:, None] * inv_freq, col[:, None] * inv_freq], axis=-1)
    return jnp.cos(ang)[:, None, :], jnp.sin(ang)[:, None, :]

def apply_rope(x, cos, sin):
    xf = x.astype(jnp.float32)
    x1, x2 = jnp.split(xf, 2, axis=-1)
    return jnp.concatenate([x1 * cos - x2 * sin, x2 * cos + x1 * sin], axis=-1).astype(x.dtype)

def sink_softmax(logits, sink):
    full = jnp.concatenate([logits, jnp.broadcast_to(sink, logits.shape[:-1] + (1,))], axis=-1)
    return jax.nn.softmax(full, axis=-1)[..., :-1]

def conv_mixers(h, w_in, conv_a, conv_b, conv_b_bias, ln_g, ln_b, w_out):
    p = h @ w_in
    g_b, g_c, u_a, v_b, gate_b = jnp.split(
        p, [A_WIDTH, 2 * A_WIDTH, 3 * A_WIDTH, 3 * A_WIDTH + B_WIDTH], axis=-1)
    y_a = g_b * dwconv(g_c * u_a, conv_a)
    u = v_b * jax.nn.sigmoid(gate_b)
    u = dwconv(u, conv_b) + conv_b_bias
    y_b = jax.nn.silu(layernorm(u, ln_g, ln_b))
    return jnp.concatenate([y_a, y_b], axis=-1) @ w_out

def windowed_gqa(h, hc, w_qkv, w_o, sinks, need_ctx_out):
    bsz, length, _ = h.shape
    n_ctx = hc.shape[1]
    scale = HEAD_DIM ** -0.5
    q, k, v = jnp.split(h @ w_qkv, [Q_W, Q_W + KV_W], axis=-1)
    q = q.reshape(bsz, length, N_HEADS, HEAD_DIM)
    k = k.reshape(bsz, length, N_KV_HEADS, HEAD_DIM)
    v = v.reshape(bsz, length, N_KV_HEADS, HEAD_DIM)
    cos, sin = axial_rope_tables(length)
    q = apply_rope(q, cos, sin) * scale
    k = apply_rope(k, cos, sin)
    kc, vc = jnp.split(hc @ w_qkv[:, Q_W:], [KV_W], axis=-1)
    kc = kc.reshape(bsz, n_ctx, N_KV_HEADS, HEAD_DIM)
    vc = vc.reshape(bsz, n_ctx, N_KV_HEADS, HEAD_DIM)
    sink = sinks.astype(jnp.float32).reshape(1, N_KV_HEADS, Q_GROUP, 1, 1)

    nblk = length // BLOCK
    qb = q.reshape(bsz, nblk, BLOCK, N_KV_HEADS, Q_GROUP, HEAD_DIM)

    def band(t):
        tb = t.reshape(bsz, nblk, BLOCK, N_KV_HEADS, HEAD_DIM)
        tp = jnp.pad(tb, ((0, 0), (1, 1), (0, 0), (0, 0), (0, 0)))
        return jnp.concatenate([tp[:, :-2], tp[:, 1:-1], tp[:, 2:]], axis=2)

    k_band, v_band = band(k), band(v)
    blk = jnp.arange(nblk)[:, None, None]
    q_pos = blk * BLOCK + jnp.arange(BLOCK)[None, :, None]
    k_pos = (blk - 1) * BLOCK + jnp.arange(3 * BLOCK)[None, None, :]
    mask = (jnp.abs(q_pos - k_pos) <= WINDOW) & (k_pos >= 0) & (k_pos < length)

    def attend_block(args):
        q_blk, k_blk, v_blk, m = args
        s_loc = jnp.einsum('bqhgd,bshd->bhgqs', q_blk, k_blk).astype(jnp.float32)
        s_loc = jnp.where(m, s_loc, NEG_INF)
        s_ctx = jnp.einsum('bqhgd,bchd->bhgqc', q_blk, kc).astype(jnp.float32)
        p = sink_softmax(jnp.concatenate([s_loc, s_ctx], axis=-1), sink)
        p_loc = p[..., :3 * BLOCK].astype(v_blk.dtype)
        p_ctx = p[..., 3 * BLOCK:].astype(vc.dtype)
        return (jnp.einsum('bhgqs,bshd->bqhgd', p_loc, v_blk)
                + jnp.einsum('bhgqc,bchd->bqhgd', p_ctx, vc))

    out = lax.map(attend_block, (jnp.moveaxis(qb, 1, 0), jnp.moveaxis(k_band, 1, 0),
                                 jnp.moveaxis(v_band, 1, 0), mask))
    y = jnp.moveaxis(out, 0, 1).reshape(bsz, length, Q_W) @ w_o

    yc = None
    if need_ctx_out:
        qc = (hc @ w_qkv[:, :Q_W]).reshape(bsz, n_ctx, N_KV_HEADS, Q_GROUP, HEAD_DIM) * scale
        s = jnp.einsum('bqhgd,bchd->bhgqc', qc, kc).astype(jnp.float32)
        p = sink_softmax(s, sink).astype(vc.dtype)
        yc = jnp.einsum('bhgqc,bchd->bqhgd', p, vc).reshape(bsz, n_ctx, Q_W) @ w_o
    return y, yc

def conv_ffn(h, w_up, conv, w_down):
    u = dwconv(h @ w_up, conv)
    a, g = jnp.split(u, 2, axis=-1)
    return (jax.nn.silu(g) * a) @ w_down

def first_inputs(seed: int = 0) -> dict:
    key = jax.random.key(seed)
    ks = jax.random.split(key, 22)

    def nrm(k, shape, s):
        return jax.random.normal(k, shape, jnp.float32) * s

    return {
        'x': nrm(ks[0], (BATCH, SEQ, D_MODEL), 1.0),
        'c': nrm(ks[1], (BATCH, D_MODEL), 1.0),
        'ctx': nrm(ks[2], (BATCH, CTX_LEN, D_MODEL), 1.0),
        'c_ctx': nrm(ks[3], (D_MODEL,), 1.0),
        'w_mod': nrm(ks[4], (DEPTH, D_MODEL, 6 * D_MODEL), 0.5 * D_MODEL ** -0.5),
        'b_mod': nrm(ks[5], (DEPTH, 6 * D_MODEL), 0.02),
        'norm_mix': 1.0 + nrm(ks[6], (DEPTH, D_MODEL), 0.02),
        'norm_ffn': 1.0 + nrm(ks[7], (DEPTH, D_MODEL), 0.02),
        'w_in_ab': nrm(ks[8], (N_EVEN, D_MODEL, AB_IN), D_MODEL ** -0.5),
        'conv_a': nrm(ks[9], (N_EVEN, A_CONV, A_WIDTH), A_CONV ** -0.5),
        'conv_b': nrm(ks[10], (N_EVEN, B_CONV, B_WIDTH), B_CONV ** -0.5),
        'conv_b_bias': nrm(ks[11], (N_EVEN, B_WIDTH), 0.02),
        'ln_b_gain': 1.0 + nrm(ks[12], (N_EVEN, B_WIDTH), 0.02),
        'ln_b_bias': nrm(ks[13], (N_EVEN, B_WIDTH), 0.02),
        'w_out_ab': nrm(ks[14], (N_EVEN, AB_OUT, D_MODEL), AB_OUT ** -0.5),
        'w_qkv': nrm(ks[15], (N_ODD, D_MODEL, Q_W + 2 * KV_W), D_MODEL ** -0.5),
        'w_o': nrm(ks[16], (N_ODD, Q_W, D_MODEL), Q_W ** -0.5),
        'sinks': nrm(ks[17], (N_ODD, N_HEADS), 1.0),
        'w_up': nrm(ks[18], (DEPTH, D_MODEL, 2 * D_FF), D_MODEL ** -0.5),
        'w_conv_ffn': nrm(ks[19], (DEPTH, FFN_CONV, 2 * D_FF), FFN_CONV ** -0.5),
        'w_down': nrm(ks[20], (DEPTH, D_FF, D_MODEL), D_FF ** -0.5),
        'final_norm': 1.0 + nrm(ks[21], (D_MODEL,), 0.02),
    }

def first_block(x, c, ctx, c_ctx, w_mod, b_mod, norm_mix, norm_ffn, w_in_ab, conv_a, conv_b,
              conv_b_bias, ln_b_gain, ln_b_bias, w_out_ab, w_qkv, w_o, sinks, w_up, w_conv_ffn,
              w_down, final_norm):
    xc = ctx
    for l in range(DEPTH):
        last = l == DEPTH - 1
        sh1, sc1, g1, sh2, sc2, g2 = adaln(c[:, None, :], w_mod[l], b_mod[l])
        csh1, csc1, cg1, csh2, csc2, cg2 = adaln(c_ctx, w_mod[l], b_mod[l])
        h = modulate(rmsnorm(x, norm_mix[l]), sh1, sc1)
        hc = modulate(rmsnorm(xc, norm_mix[l]), csh1, csc1)
        if l % 2 == 0:
            e = l // 2
            y = conv_mixers(h, w_in_ab[e], conv_a[e], conv_b[e], conv_b_bias[e],
                            ln_b_gain[e], ln_b_bias[e], w_out_ab[e])
            yc = None if last else conv_mixers(hc, w_in_ab[e], conv_a[e], conv_b[e], conv_b_bias[e],
                                               ln_b_gain[e], ln_b_bias[e], w_out_ab[e])
        else:
            o = l // 2
            y, yc = windowed_gqa(h, hc, w_qkv[o], w_o[o], sinks[o], not last)
        x = x + g1 * y
        x = x + g2 * conv_ffn(modulate(rmsnorm(x, norm_ffn[l]), sh2, sc2), w_up[l], w_conv_ffn[l], w_down[l])
        if not last:
            xc = xc + cg1 * yc
            xc = xc + cg2 * conv_ffn(modulate(rmsnorm(xc, norm_ffn[l]), csh2, csc2),
                                     w_up[l], w_conv_ffn[l], w_down[l])
    return rmsnorm(x, final_norm)


DEPTH_2 = 1

SSM_D_INNER = D_MODEL
SSM_HEAD_DIM = 64
SSM_HEADS = SSM_D_INNER // SSM_HEAD_DIM
SSM_GROUPS = 4
SSM_D_STATE = 128
SSM_CONV = 4
SSM_CHUNK = 128
SSM_CONV_DIM = SSM_D_INNER + 2 * SSM_GROUPS * SSM_D_STATE
SB_HEAD_DIM = 128
SB_HEADS = 4
SB_QBLK = 128
NSA_HEAD_DIM = 64
NSA_Q_HEADS = 8
NSA_KV_HEADS = 2
CMP_STRIDE = 16
CMP_LEN = 2 * CMP_STRIDE
SEL_BLOCK = 64
N_SEL = 8
WINDOW_2 = 512
NSA_QBLK = 32
D_FF_2 = 11 * D_MODEL // 4

NORM_EPS = 1e-6
NEG = -1e30
BIG = 1e30

IN_SPLIT_SIZES = (SSM_D_INNER, SSM_CONV_DIM, SSM_HEADS, 3 * SB_HEADS * SB_HEAD_DIM,
                  NSA_Q_HEADS * NSA_HEAD_DIM, 6 * NSA_KV_HEADS * NSA_HEAD_DIM, 3 * NSA_Q_HEADS, 3 * D_MODEL)
D_IN = sum(IN_SPLIT_SIZES)


def rms_norm(x, w):
    xf = x.astype(jnp.float32)
    y = xf * lax.rsqrt(jnp.mean(xf * xf, axis=-1, keepdims=True) + NORM_EPS)
    return (y * w.astype(jnp.float32)).astype(x.dtype)

def causal_dwconv(x, w, b):
    k, c = w.shape
    out = lax.conv_general_dilated(x, w[:, None, :].astype(x.dtype), window_strides=(1,),
                                   padding=[(k - 1, 0)], dimension_numbers=('NWC', 'WIO', 'NWC'),
                                   feature_group_count=c)
    return out + b.astype(x.dtype)

def masked_softmax(s, mask):
    p = jax.nn.softmax(jnp.where(mask, s, NEG), axis=-1)
    return jnp.where(mask, p, 0.0)

def alibi_slopes(n):
    return jnp.asarray(2.0 ** (-8.0 * np.arange(1, n + 1) / n), dtype=jnp.float32)

def split_points():
    return np.cumsum(np.array(IN_SPLIT_SIZES))[:-1].tolist()

def ssd_chunked(x, dt, a, bmat, cmat):
    bsz, s, h, p = x.shape
    g, n = bmat.shape[2], bmat.shape[3]
    hg = h // g
    nc = s // SSM_CHUNK

    def chunks(t, tail):
        return jnp.moveaxis(t.reshape((bsz, nc, SSM_CHUNK) + tail), 1, 0)

    xc = chunks(x, (g, hg, p))
    dtc = chunks(dt, (g, hg))
    bc = chunks(bmat, (g, n))
    cc = chunks(cmat, (g, n))
    a = a.reshape(g, hg)
    tri = jnp.tril(jnp.ones((SSM_CHUNK, SSM_CHUNK), dtype=bool))[None, :, :, None, None]

    def step(state, inp):
        x_c, dt_c, b_c, c_c = inp
        acum = jnp.cumsum(dt_c * a, axis=1)
        seg = acum[:, :, None] - acum[:, None, :]
        decay = jnp.exp(jnp.where(tri, seg, -jnp.inf))
        cb = jnp.einsum('btgn,bsgn->btsg', c_c, b_c)
        w = cb[..., None] * decay * dt_c[:, None]
        y = jnp.einsum('btsgh,bsghp->btghp', w, x_c)
        y = y + jnp.einsum('btgn,bghpn->btghp', c_c, state) * jnp.exp(acum)[..., None]
        to_end = jnp.exp(acum[:, -1:] - acum) * dt_c
        state = (state * jnp.exp(acum[:, -1])[..., None, None]
                 + jnp.einsum('bsgh,bsghp,bsgn->bghpn', to_end, x_c, b_c))
        return state, y

    state0 = jnp.zeros((bsz, g, hg, p, n), jnp.float32)
    _, ys = lax.scan(step, state0, (xc, dtc, bc, cc))
    return jnp.moveaxis(ys, 0, 1).reshape(bsz, s, h, p)

def ssm_mixer(z, xbc, dt_raw, conv_w, conv_b, dt_bias, a_log, d_skip, norm_w):
    bsz, s, _ = z.shape
    xbc = jax.nn.silu(causal_dwconv(xbc, conv_w, conv_b))
    xs, bm, cm = jnp.split(xbc, [SSM_D_INNER, SSM_D_INNER + SSM_GROUPS * SSM_D_STATE], axis=-1)
    xs = xs.reshape(bsz, s, SSM_HEADS, SSM_HEAD_DIM).astype(jnp.float32)
    bm = bm.reshape(bsz, s, SSM_GROUPS, SSM_D_STATE).astype(jnp.float32)
    cm = cm.reshape(bsz, s, SSM_GROUPS, SSM_D_STATE).astype(jnp.float32)
    dt = jax.nn.softplus(dt_raw.astype(jnp.float32) + dt_bias.astype(jnp.float32))
    a = -jnp.exp(a_log.astype(jnp.float32))
    y = ssd_chunked(xs, dt, a, bm, cm) + d_skip.astype(jnp.float32)[:, None] * xs
    y = y.reshape(bsz, s, SSM_D_INNER) * jax.nn.silu(z.astype(jnp.float32))
    yg = y.reshape(bsz, s, SSM_GROUPS, SSM_D_INNER // SSM_GROUPS)
    yg = yg * lax.rsqrt(jnp.mean(yg * yg, axis=-1, keepdims=True) + NORM_EPS)
    return (yg.reshape(bsz, s, SSM_D_INNER) * norm_w.astype(jnp.float32)).astype(z.dtype)

def stick_breaking_attention(qkv):
    bsz, s, _ = qkv.shape
    q, k, v = [jnp.moveaxis(t.reshape(bsz, s, SB_HEADS, SB_HEAD_DIM), 2, 1)
               for t in jnp.split(qkv, 3, axis=-1)]
    scale = SB_HEAD_DIM ** -0.5
    outs = []
    for i in range(s // SB_QBLK):
        q0 = i * SB_QBLK
        kl = q0 + SB_QBLK
        qb = q[:, :, q0:kl]
        zl = jnp.einsum('bhqd,bhkd->bhqk', qb, k[:, :, :kl]).astype(jnp.float32) * scale
        mask = jnp.arange(kl)[None, :] < (q0 + jnp.arange(SB_QBLK))[:, None]
        ls = jax.nn.log_sigmoid(zl)
        lk = jnp.where(mask, ls - zl, 0.0)
        later = lax.cumsum(lk, axis=3, reverse=True) - lk
        w = jnp.where(mask, jnp.exp(ls + later), 0.0)
        outs.append(jnp.einsum('bhqk,bhkd->bhqd', w.astype(v.dtype), v[:, :, :kl]))
    out = jnp.concatenate(outs, axis=2)
    return out.transpose(0, 2, 1, 3).reshape(bsz, s, SB_HEADS * SB_HEAD_DIM)

def compress_blocks(kraw, pos_emb, w1, w2):
    bsz, s, g, dh = kraw.shape
    chunks = kraw.reshape(bsz, s // CMP_STRIDE, CMP_STRIDE, g, dh)
    blocks = jnp.concatenate([chunks[:, :-1], chunks[:, 1:]], axis=2) + pos_emb[None, None, :, None, :].astype(kraw.dtype)
    blocks = blocks.transpose(0, 1, 3, 2, 4).reshape(bsz, s // CMP_STRIDE - 1, g, CMP_LEN * dh)
    return jax.nn.silu(blocks @ w1) @ w2

def nsa_attention(q, kv, gate, cmp_pos_k, cmp_w1_k, cmp_w2_k, cmp_pos_v, cmp_w1_v, cmp_w2_v):
    bsz, s, _ = q.shape
    g, hg, dh = NSA_KV_HEADS, NSA_Q_HEADS // NSA_KV_HEADS, NSA_HEAD_DIM
    q = q.reshape(bsz, s, g, hg, dh)
    k_cmp, v_cmp, k_sel, v_sel, k_win, v_win = [t.reshape(bsz, s, g, dh) for t in jnp.split(kv, 6, axis=-1)]
    gate = jax.nn.sigmoid(gate.astype(jnp.float32)).reshape(bsz, s, 3, g, hg)
    kc = compress_blocks(k_cmp, cmp_pos_k, cmp_w1_k, cmp_w2_k)
    vc = compress_blocks(v_cmp, cmp_pos_v, cmp_w1_v, cmp_w2_v)
    nc = kc.shape[1]
    cmp_end = jnp.arange(nc) * CMP_STRIDE + CMP_LEN - 1
    nb = s // SEL_BLOCK
    n_sel = min(N_SEL, nb)
    ratio = SEL_BLOCK // CMP_STRIDE
    ks_blk = k_sel.reshape(bsz, nb, SEL_BLOCK, g, dh).transpose(0, 3, 1, 2, 4)
    vs_blk = v_sel.reshape(bsz, nb, SEL_BLOCK, g, dh).transpose(0, 3, 1, 2, 4)
    kw = jnp.pad(k_win, ((0, 0), (WINDOW_2, 0), (0, 0), (0, 0)))
    vw = jnp.pad(v_win, ((0, 0), (WINDOW_2, 0), (0, 0), (0, 0)))
    slopes = alibi_slopes(NSA_Q_HEADS).reshape(g, hg)
    scale = dh ** -0.5
    bi = jnp.arange(bsz)[:, None, None, None]
    gi = jnp.arange(g)[None, :, None, None]
    blk_ids = jnp.arange(nb)

    def block(q0):
        qb = lax.dynamic_slice_in_dim(q, q0, NSA_QBLK, axis=1)
        gb = lax.dynamic_slice_in_dim(gate, q0, NSA_QBLK, axis=1)
        tpos = q0 + jnp.arange(NSA_QBLK)
        dist_c = tpos[:, None] - cmp_end[None, :]
        sc = (jnp.einsum('bqghd,bngd->bghqn', qb, kc).astype(jnp.float32) * scale
              - slopes[:, :, None, None] * dist_c.astype(jnp.float32))
        p_cmp = masked_softmax(sc, dist_c >= 0)
        o_cmp = jnp.einsum('bghqn,bngd->bqghd', p_cmp.astype(vc.dtype), vc)
        imp_pad = jnp.pad(p_cmp.sum(axis=2), ((0, 0), (0, 0), (0, 0), (1, 0)))
        imp = (imp_pad.reshape(bsz, g, NSA_QBLK, nb, ratio).sum(axis=-1)
               + jnp.pad(imp_pad[..., ratio::ratio], ((0, 0), (0, 0), (0, 0), (0, 1))))
        cur = tpos // SEL_BLOCK
        forced = ((blk_ids[None, :] == 0) | (blk_ids[None, :] == cur[:, None])
                  | (blk_ids[None, :] == cur[:, None] - 1))
        valid = blk_ids[None, :] * SEL_BLOCK <= tpos[:, None]
        imp = jnp.where(valid, jnp.where(forced, BIG, imp), NEG)
        _, idx = lax.top_k(imp, n_sel)
        ks = ks_blk[bi, gi, idx]
        vs = vs_blk[bi, gi, idx]
        pos = idx[..., None] * SEL_BLOCK + jnp.arange(SEL_BLOCK)
        dist_s = tpos[None, None, :, None, None] - pos
        ss = (jnp.einsum('bqghd,bgqnkd->bghqnk', qb, ks).astype(jnp.float32) * scale
              - slopes[None, :, :, None, None, None] * dist_s[:, :, None].astype(jnp.float32))
        ss = ss.reshape(bsz, g, hg, NSA_QBLK, n_sel * SEL_BLOCK)
        p_sel = masked_softmax(ss, (dist_s >= 0).reshape(bsz, g, 1, NSA_QBLK, n_sel * SEL_BLOCK))
        o_sel = jnp.einsum('bghqm,bgqmd->bqghd', p_sel.astype(vs.dtype),
                           vs.reshape(bsz, g, NSA_QBLK, n_sel * SEL_BLOCK, dh))
        kwb = lax.dynamic_slice_in_dim(kw, q0, WINDOW_2 + NSA_QBLK, axis=1)
        vwb = lax.dynamic_slice_in_dim(vw, q0, WINDOW_2 + NSA_QBLK, axis=1)
        wpos = q0 - WINDOW_2 + jnp.arange(WINDOW_2 + NSA_QBLK)
        dist_w = tpos[:, None] - wpos[None, :]
        wmask = (dist_w >= 0) & (dist_w < WINDOW_2) & (wpos[None, :] >= 0)
        sw = (jnp.einsum('bqghd,bkgd->bghqk', qb, kwb).astype(jnp.float32) * scale
              - slopes[:, :, None, None] * dist_w.astype(jnp.float32))
        o_win = jnp.einsum('bghqk,bkgd->bqghd', masked_softmax(sw, wmask).astype(vwb.dtype), vwb)
        out = (gb[:, :, 0, :, :, None] * o_cmp + gb[:, :, 1, :, :, None] * o_sel
               + gb[:, :, 2, :, :, None] * o_win)
        return out.astype(q.dtype)

    out = lax.map(block, jnp.arange(0, s, NSA_QBLK))
    return jnp.moveaxis(out, 0, 1).reshape(bsz, s, NSA_Q_HEADS * NSA_HEAD_DIM)

def second_inputs(seed: int = 0) -> dict:
    key = jax.random.key(seed)
    ks = iter(jax.random.split(key, 40))
    L = DEPTH_2
    f32 = jnp.float32

    def nrm(shape, scale):
        return jax.random.normal(next(ks), shape, f32) * scale

    def gain(shape):
        return 1.0 + nrm(shape, 0.02)

    dt0 = jnp.exp(jax.random.uniform(next(ks), (L, SSM_HEADS), f32)
                  * (math.log(0.1) - math.log(1e-3)) + math.log(1e-3))
    dt_bias = dt0 + jnp.log(-jnp.expm1(-dt0))
    a_log = jnp.log(jax.random.uniform(next(ks), (L, SSM_HEADS), f32, minval=1.0, maxval=16.0))
    return {
        "x": nrm((BATCH, SEQ, D_MODEL), 1.0),
        "pre_mix_norm": gain((L, D_MODEL)),
        "w_in": nrm((L, D_MODEL, D_IN), D_MODEL ** -0.5),
        "ssm_conv_w": nrm((L, SSM_CONV, SSM_CONV_DIM), SSM_CONV ** -0.5),
        "ssm_conv_b": nrm((L, SSM_CONV_DIM), 0.01),
        "ssm_dt_bias": dt_bias,
        "ssm_a_log": a_log,
        "ssm_d": 1.0 + nrm((L, SSM_HEADS), 0.1),
        "ssm_norm": gain((L, SSM_D_INNER)),
        "cmp_pos_k": nrm((L, CMP_LEN, NSA_HEAD_DIM), 0.02),
        "cmp_w1_k": nrm((L, CMP_LEN * NSA_HEAD_DIM, NSA_HEAD_DIM), (CMP_LEN * NSA_HEAD_DIM) ** -0.5),
        "cmp_w2_k": nrm((L, NSA_HEAD_DIM, NSA_HEAD_DIM), NSA_HEAD_DIM ** -0.5),
        "cmp_pos_v": nrm((L, CMP_LEN, NSA_HEAD_DIM), 0.02),
        "cmp_w1_v": nrm((L, CMP_LEN * NSA_HEAD_DIM, NSA_HEAD_DIM), (CMP_LEN * NSA_HEAD_DIM) ** -0.5),
        "cmp_w2_v": nrm((L, NSA_HEAD_DIM, NSA_HEAD_DIM), NSA_HEAD_DIM ** -0.5),
        "w_br_ssm": nrm((L, SSM_D_INNER, D_MODEL), SSM_D_INNER ** -0.5),
        "w_br_sb": nrm((L, SB_HEADS * SB_HEAD_DIM, D_MODEL), (SB_HEADS * SB_HEAD_DIM) ** -0.5),
        "w_br_nsa": nrm((L, NSA_Q_HEADS * NSA_HEAD_DIM, D_MODEL), (NSA_Q_HEADS * NSA_HEAD_DIM) ** -0.5),
        "w_out": nrm((L, D_MODEL, D_MODEL), D_MODEL ** -0.5),
        "post_mix_norm": gain((L, D_MODEL)),
        "pre_ffn_norm": gain((L, D_MODEL)),
        "ffn_w_up": nrm((L, D_MODEL, 2 * D_FF_2), D_MODEL ** -0.5),
        "ffn_conv_w": nrm((L, FFN_CONV, 2 * D_FF_2), FFN_CONV ** -0.5),
        "ffn_conv_b": nrm((L, 2 * D_FF_2), 0.01),
        "ffn_w_down": nrm((L, D_FF_2, D_MODEL), D_FF_2 ** -0.5),
        "post_ffn_norm": gain((L, D_MODEL)),
    }

def second_block(x, pre_mix_norm, w_in, ssm_conv_w, ssm_conv_b, ssm_dt_bias, ssm_a_log, ssm_d, ssm_norm,
              cmp_pos_k, cmp_w1_k, cmp_w2_k, cmp_pos_v, cmp_w1_v, cmp_w2_v,
              w_br_ssm, w_br_sb, w_br_nsa, w_out, post_mix_norm, pre_ffn_norm,
              ffn_w_up, ffn_conv_w, ffn_conv_b, ffn_w_down, post_ffn_norm):
    bsz, s, _ = x.shape
    for l in range(DEPTH_2):
        h = rms_norm(x, pre_mix_norm[l])
        proj = h @ w_in[l]
        z, xbc, dt_raw, sb_qkv, nsa_q, nsa_kv, nsa_gate, merge_gate = jnp.split(proj, split_points(), axis=-1)
        y_ssm = ssm_mixer(z, xbc, dt_raw, ssm_conv_w[l], ssm_conv_b[l], ssm_dt_bias[l],
                          ssm_a_log[l], ssm_d[l], ssm_norm[l])
        y_sb = stick_breaking_attention(sb_qkv)
        y_nsa = nsa_attention(nsa_q, nsa_kv, nsa_gate, cmp_pos_k[l], cmp_w1_k[l], cmp_w2_k[l],
                              cmp_pos_v[l], cmp_w1_v[l], cmp_w2_v[l])
        gm = jax.nn.sigmoid(merge_gate.astype(jnp.float32)).reshape(bsz, s, 3, D_MODEL)
        mixed = (gm[:, :, 0] * (y_ssm @ w_br_ssm[l]) + gm[:, :, 1] * (y_sb @ w_br_sb[l])
                 + gm[:, :, 2] * (y_nsa @ w_br_nsa[l])).astype(x.dtype)
        x = x + rms_norm(mixed @ w_out[l], post_mix_norm[l])
        h = rms_norm(x, pre_ffn_norm[l])
        u = causal_dwconv(h @ ffn_w_up[l], ffn_conv_w[l], ffn_conv_b[l])
        gate, val = jnp.split(u, 2, axis=-1)
        f = (jax.nn.gelu(gate, approximate=True) * val) @ ffn_w_down[l]
        x = x + rms_norm(f, post_ffn_norm[l])
    return x


def setup_inputs(seed=0):
    out = dict(first_inputs(seed))
    for name, value in second_inputs(seed + 1).items():
        if name != "x":
            out[name + "_2"] = value
    return out


def reference(
    x, c, ctx, c_ctx, w_mod, b_mod, norm_mix, norm_ffn, w_in_ab, conv_a, conv_b, conv_b_bias,
    ln_b_gain, ln_b_bias, w_out_ab, w_qkv, w_o, sinks, w_up, w_conv_ffn, w_down, final_norm,
    pre_mix_norm_2, w_in_2, ssm_conv_w_2, ssm_conv_b_2, ssm_dt_bias_2, ssm_a_log_2, ssm_d_2,
    ssm_norm_2, cmp_pos_k_2, cmp_w1_k_2, cmp_w2_k_2, cmp_pos_v_2, cmp_w1_v_2, cmp_w2_v_2,
    w_br_ssm_2, w_br_sb_2, w_br_nsa_2, w_out_2, post_mix_norm_2, pre_ffn_norm_2, ffn_w_up_2,
    ffn_conv_w_2, ffn_conv_b_2, ffn_w_down_2, post_ffn_norm_2,
):
    x = first_block(
        x, c, ctx, c_ctx, w_mod, b_mod, norm_mix, norm_ffn, w_in_ab, conv_a, conv_b,
        conv_b_bias, ln_b_gain, ln_b_bias, w_out_ab, w_qkv, w_o, sinks, w_up, w_conv_ffn,
        w_down, final_norm,
    )
    return second_block(
        x, pre_mix_norm_2, w_in_2, ssm_conv_w_2, ssm_conv_b_2, ssm_dt_bias_2, ssm_a_log_2,
        ssm_d_2, ssm_norm_2, cmp_pos_k_2, cmp_w1_k_2, cmp_w2_k_2, cmp_pos_v_2, cmp_w1_v_2,
        cmp_w2_v_2, w_br_ssm_2, w_br_sb_2, w_br_nsa_2, w_out_2, post_mix_norm_2, pre_ffn_norm_2,
        ffn_w_up_2, ffn_conv_w_2, ffn_conv_b_2, ffn_w_down_2, post_ffn_norm_2,
    )


_drawn_inputs = setup_inputs


def setup_inputs(seed=0):
    import zlib

    import numpy as np

    out = dict(_drawn_inputs(seed))
    spreads = {}
    factors = {'norm_mix': 3.835,
     'norm_ffn': 4.564,
     'conv_b_bias': 31.07,
     'ln_b_gain': 64.0,
     'ln_b_bias': 64.0,
     'sinks': 64.0,
     'ssm_conv_b_2': 6.137,
     'ssm_norm_2': 4.276,
     'cmp_pos_k_2': 64.0,
     'cmp_pos_v_2': 35.92,
     'post_mix_norm_2': 3.132,
     'pre_ffn_norm_2': 3.379,
     'ffn_conv_b_2': 6.973,
     'post_ffn_norm_2': 47.838,
     'cmp_w1_k_2': 4.29,
     'cmp_w2_k_2': 4.15}
    for name, (base, spread) in spreads.items():
        noise = np.random.default_rng([zlib.crc32(name.encode()), seed]).standard_normal(out[name].shape)
        drawn = base * np.exp(spread * noise) if base else spread * noise
        out[name] = __import__('jax').numpy.asarray(drawn.astype(out[name].dtype))
    for name, factor in factors.items():
        out[name] = (out[name] * factor).astype(out[name].dtype)
    return out
```

```python
import numpy as np
import concourse.bass as bass
from concourse import mybir
from concourse.alu_op_type import AluOpType as ALU

ACT = mybir.ActivationFunctionType
F32 = mybir.dt.float32
F32R = mybir.dt.float32r
AX = mybir.AxisListType

P = 128
D = 1024
KD = D // P
TX, TC = 512, 256
TALL = TX + TC
SEG_BOTH = ((0, TX), (TX, TC))
SEG_X = ((0, TX),)
EPS = 1e-6
NEG = -1e30
FF = 2816
FFT = FF // P
HALF = FFT // 2
SLOT = HALF * P

AW = 512
HD = 64
NH, NKV = 16, 4
BLK = 128
NBLK = TX // BLK
GRID_W = 64

SSM_H, SSM_G, SSM_N, SSM_P = 16, 4, 128, 64
SB_H = 4
NSA_H, NSA_G = 8, 2
CMP_STRIDE, CMP_LEN = 16, 32
NCMP = TX // CMP_STRIDE - 1
SLOPES = [2.0 ** (-8.0 * (h + 1) / NSA_H) for h in range(NSA_H)]

PARAM_COLS = [
    ("cond", 2 * KD), ("b_mod", 2 * 48), ("norm_mix", 2 * KD), ("norm_ffn", 2 * KD),
    ("conv_a", 3 * 4), ("conv_b", 31 * 4), ("conv_b_bias", 4), ("ln_g", 4), ("ln_b", 4),
    ("conv_ffn", 2 * 3 * 44), ("final_norm", KD), ("pre_mix", KD), ("ssm_conv_w", 4 * 16),
    ("ssm_conv_b", 16), ("ssm_norm", KD), ("post_mix", KD), ("pre_ffn", KD),
    ("conv_ffn2", 3 * 44), ("conv_ffn2_b", 44), ("post_ffn", KD),
    ("dt_bias", 16), ("a_log", 16), ("ssm_d", 16), ("sinks", 16), ("eps", 1),
]
CONST_COLS = [
    ("ident", 128), ("upto", 128), ("later", 128), ("neg_from", 128),
    ("neg_one", 128), ("before", 128), ("pick", 2),
    ("rope_rot", 128), ("cos", 512), ("sin", 512), ("window", 384),
    ("dist", 512), ("cmp_dist", 4 * NCMP), ("cmp_valid", 4 * NCMP),
]


def columns(table):
    at, out = 0, {}
    for name, width in table:
        out[name] = (at, width)
        at += width
    return out, at


PCOL, NPARAM = columns(PARAM_COLS)
CCOL, NCONST = columns(CONST_COLS)

WEIGHTS = {
    "mod": (2 * 48, 2, 512), "in_ab": (20, 8, 128), "out_ab": (8, 8, 128), "up": (88, 8, 128),
    "down": (32, HALF, 128), "qk": (10, 8, 128), "v": (2, 4, 256), "o": (8, 8, 128),
    "z": (8, 2, 512), "xbc": (16, 8, 128), "dtg": (1, 8, 40), "sbqk": (8, 8, 128),
    "sbv": (4, 2, 512), "nq": (4, 8, 128), "nk": (4, 8, 128), "nv": (2, 4, 256),
    "gate": (24, 8, 128), "br_ssm": (8, 8, 128), "br_sb": (8, 4, 128), "br_nsa": (8, 4, 128),
    "out2": (8, 8, 128), "up2": (44, 8, 128), "down2": (16, HALF, 128),
}


def weight_plan():
    plan = []

    def ffn(up, down, layer):
        for half in range(2):
            for t in range(HALF):
                plan.append((up, layer * 44 + half * HALF + t))
                plan.append((up, layer * 44 + FFT + half * HALF + t))
            plan.extend((down, layer * 16 + half * 8 + m) for m in range(KD))

    plan += [("mod", i) for i in range(48)]
    for t in range(4):
        plan += [("in_ab", 12 + t), ("in_ab", 16 + t)]
    for t in range(4):
        plan += [("in_ab", 4 + t), ("in_ab", 8 + t), ("in_ab", t)]
    plan += [("out_ab", m) for m in range(KD)]
    ffn("up", "down", 0)
    plan += [("mod", 48 + i) for i in range(48)]
    plan += [("v", 0), ("v", 1)] + [("qk", m) for m in (8, 9, *range(8))]
    plan += [("o", m) for m in range(KD)]
    ffn("up", "down", 1)
    plan += [("dtg", 0)] + [("xbc", m) for m in range(16)] + [("z", i) for i in range(8)]
    plan += [("sbqk", m) for m in range(8)] + [("sbv", i) for i in range(4)]
    plan += [("nk", m) for m in range(4)] + [("nv", 0), ("nv", 1)] + [("nq", m) for m in range(4)]
    for m in range(KD):
        plan += [("gate", m), ("br_ssm", m), ("gate", 8 + m), ("br_sb", m),
                 ("gate", 16 + m), ("br_nsa", m)]
    plan += [("out2", m) for m in range(KD)]
    ffn("up2", "down2", 0)
    return plan


class Engine:

    def __init__(self, nc, eng, name):
        self.eng = eng
        self.sem = nc.alloc_semaphore(f"done_{name}")
        self.count = 0
        self.waited = {}

    def after(self, *tokens):
        for tok in tokens:
            if tok is None:
                continue
            sem, value = tok
            if self.waited.get(id(sem), 0) < value:
                self.eng.wait_ge(sem, value)
                self.waited[id(sem)] = value

    def do(self, method, *args, after=(), **kw):
        self.after(*after)
        ins = method(*args, **kw)
        ins.then_inc(self.sem, 1)
        self.count += 1
        return (self.sem, self.count)


class Turn:

    def __init__(self, aps):
        self.aps = aps
        self.at = 0

    def next(self):
        i = self.at % len(self.aps)
        self.at += 1
        return i, self.aps[i]


def build(nc, dram, out):
    pe = Engine(nc, nc.tensor, "pe")
    act = Engine(nc, nc.scalar, "act")
    dve = Engine(nc, nc.vector, "dve")
    pool = Engine(nc, nc.gpsimd, "pool")
    V, S, T, G = nc.vector, nc.scalar, nc.tensor, nc.gpsimd

    def sbuf(name, cols, dt=F32):
        return nc.alloc_sbuf_tensor(name, [P, cols], dt)[:, :]

    params = sbuf("params", NPARAM)
    resident = CCOL["rope_rot"][0]
    consts = sbuf("consts", resident)
    mod = sbuf("mod", 96).rearrange("p (c w) -> p c w", w=2)
    gain = sbuf("gain", 2 * KD).rearrange("p (k w) -> p k w", w=2)
    ssm_small = sbuf("ssm_small", 360)
    mean_ones = sbuf("mean_ones", P)
    rstd = sbuf("rstd", TALL)
    NRAW, NHALF = 3, 2
    raw = [sbuf(f"w_raw{i}", SLOT) for i in range(NRAW)]
    w_hi = [sbuf(f"w_hi{i}", SLOT, F32R) for i in range(NHALF)]
    w_lo = [sbuf(f"w_lo{i}", SLOT, F32R) for i in range(NHALF)]
    scratch = Turn([sbuf(f"scratch{i}", TALL) for i in range(5)])
    psum = nc.alloc_psum_tensor("psum", [P, 8 * 512], F32)[:, :]
    scratch_read = [()] * 5
    bank_read = [()] * 8
    bank_at = [0]

    def next_banks(n=1, among=8):
        i = (bank_at[0] + n - 1) // n * n % (among // n * n)
        bank_at[0] = i + n
        return i, bank_cols(i, n)

    def bank_cols(i, n=1):
        return psum[:, i * 512:(i + n) * 512]


    free_at = [(nc.sbuf_base + 63) // 64 * 64]
    top = nc.sbuf_usable_end

    def place(name, cols, dt=F32, at=None):
        where = free_at[0] if at is None else at
        assert where + 4 * cols <= top, (name, where + 4 * cols - top)
        if at is None:
            free_at[0] = (where + 4 * cols + 31) // 32 * 32
        return nc.alloc_sbuf_tensor_at(name, [P, cols], dt, offset=where)[:, :]

    def tiles(ap, width):
        return ap.rearrange("p (k t) -> p k t", t=width)

    x_at = free_at[0]
    xall = tiles(place("xall", KD * TALL), TALL)
    h_at = free_at[0]
    h_hi = tiles(place("h_hi", KD * TALL, F32R), TALL)
    h_lo = tiles(place("h_lo", KD * TALL, F32R), TALL)
    arena = free_at[0]

    def param(name, i=0, n=1):
        at, _ = PCOL[name]
        return params[:, at + i:at + i + n]

    def const(name):
        at, n = CCOL[name]
        return consts[:, at:at + n]

    def f32(ap):
        return ap.bitcast(F32)

    dma_in = nc.alloc_semaphore("loaded_inputs")
    n_in = [0]

    def load(dst, src, after=()):
        pool.after(*after)
        if n_in[0]:
            pool.after((dma_in, 16 * n_in[0]))
        G.dma_start(dst, src).then_inc(dma_in, 16)
        n_in[0] += 1
        return (dma_in, 16 * n_in[0])

    p_in = load(params, dram["params"])
    c_in = load(consts, dram["consts"][:, 0:resident])
    x_in = load(xall, dram["x"].rearrange("k p t -> p k t"))
    ident = const("ident")
    ones_ready = dve.do(V.memset, mean_ones, 1.0 / D)
    for e in (pe, act, dve):
        e.after(p_in, c_in, x_in, ones_ready)

    plan = weight_plan()
    raw_sem = [nc.alloc_semaphore(f"loaded_raw{i}") for i in range(NRAW)]
    raw_read = []
    split = []
    used = []

    def split_piece(i):
        name, _ = plan[i]
        _, kt, n = WEIGHTS[name]
        r, q = i % NRAW, i % NHALF
        arrived = (raw_sem[r], 16 * (i // NRAW + 1))
        reuse = (used[i - NHALF],) if i >= NHALF else ()
        a = act.do(S.copy, w_hi[q][:, 0:kt * n], raw[r][:, 0:kt * n], after=(arrived, *reuse))
        b = dve.do(V.tensor_tensor, w_lo[q][:, 0:kt * n], raw[r][:, 0:kt * n],
                   f32(w_hi[q][:, 0:kt * n]), ALU.subtract, after=(arrived, a, *reuse))
        split.append((a, b))
        raw_read.append((a, b))

    next_piece = [0]

    def weight(name, idx):
        i = next_piece[0]
        next_piece[0] += 1
        assert plan[i] == (name, idx), (plan[i], name, idx)
        while len(split) < min(i + 2, len(plan)):
            split_piece(len(split))
        pe.after(*split[i])
        _, kt, n = WEIGHTS[name]
        q = i % NHALF
        return (w_hi[q][:, 0:kt * n].rearrange("p (k n) -> p k n", n=n),
                w_lo[q][:, 0:kt * n].rearrange("p (k n) -> p k n", n=n))

    def done_with_piece(tok):
        used.append(tok)

    def three_pass(dst, kt, stationary, moving, first=True, last=True):
        for k in range(kt):
            s_hi, s_lo = stationary(k)
            m_hi, m_lo = moving(k)
            for n, (a, b) in enumerate(((s_hi, m_hi), (s_hi, m_lo), (s_lo, m_hi))):
                start, stop = first and k == 0 and n == 0, last and k == kt - 1 and n == 2
                if stop:
                    return pe.do(T.matmul, dst, a, b, start=start, stop=True)
                if k == kt - 1 and n == 2:
                    return pe.do(T.matmul, dst, a, b, start=start, stop=False)
                T.matmul(dst, a, b, start=start, stop=False)

    def product(name, idx, acts, segs, dst, after=()):
        _, kt, _ = WEIGHTS[name]
        a_hi, a_lo = acts
        hi, lo = weight(name, idx)
        pe.after(*after)
        for t0, n in segs:
            tok = three_pass(dst[:, t0:t0 + n], kt, lambda k: (hi[:, k, :], lo[:, k, :]),
                             lambda k: (a_hi[:, k, t0:t0 + n], a_lo[:, k, t0:t0 + n]))
        done_with_piece(tok)
        return tok

    def product_tokens(name, first_idx, acts, blocks, n, dsts, after=()):
        _, kt, _ = WEIGHTS[name]
        a_hi, a_lo = acts
        pieces = KD // kt
        pe.after(*after)
        for g in range(pieces):
            hi, lo = weight(name, first_idx + g)
            for b, dst in zip(blocks, dsts):
                cols = slice(b * BLK, (b + 1) * BLK)
                tok = three_pass(dst, kt,
                                 lambda k: (a_hi[:, g * kt + k, cols], a_lo[:, g * kt + k, cols]),
                                 lambda k: (hi[:, k, :], lo[:, k, :]),
                                 first=g == 0, last=g == pieces - 1)
            done_with_piece(tok)
        return tok

    def split_acts(dst_hi, dst_lo, src, after):
        a = act.do(S.copy, dst_hi, src, after=after)
        b = dve.do(V.tensor_tensor, dst_lo, src, f32(dst_hi), ALU.subtract, after=(a, *after))
        return a, b

    rstd_readers = [()]

    def mean_of_squares(src, kt, segs, ready):
        width = segs[-1][0] + segs[-1][1]
        bank, ps = next_banks(2)
        pe.after(*bank_read[bank], *bank_read[bank + 1])
        for k in range(kt):
            i, sq = scratch.next()
            act.after(*scratch_read[i])
            a = act.do(S.activation, sq[:, 0:width], src(k), ACT.Square, after=(ready(k),))
            pe.after(a)
            for t0, n in segs:
                tok = pe.do(T.matmul, ps[:, t0:t0 + n], mean_ones, sq[:, t0:t0 + n],
                            start=k == 0, stop=k == kt - 1)
            scratch_read[i] = (tok,)
        act.after(*rstd_readers[0])
        dve.after(*rstd_readers[0])
        a = act.do(S.activation, rstd[:, 0:width], ps[:, 0:width], ACT.Sqrt, bias=param("eps"),
                   after=(tok,))
        bank_read[bank] = bank_read[bank + 1] = (a,)
        return dve.do(V.reciprocal, rstd[:, 0:width], rstd[:, 0:width], after=(a,))

    def modulated_norm(norm, layer, part, segs, ready):
        n0 = PCOL[norm][0] + layer * KD
        g = params[:, n0:n0 + KD].unsqueeze(2).broadcast_to([P, KD, 2])
        tg = dve.do(V.scalar_tensor_tensor, gain, mod[:, (part + 1) * 8:(part + 2) * 8, :], 1.0, g,
                    ALU.add, ALU.mult, after=(mod_ready[0], *gain_readers[0]))
        r = mean_of_squares(lambda k: xall[:, k, 0:segs[-1][0] + segs[-1][1]], KD, segs,
                            lambda k: ready)
        done = []
        for k in range(KD):
            i, t = scratch.next()
            dve.after(*scratch_read[i])
            for who, (t0, n) in enumerate(segs):
                shift = mod[:, part * 8 + k, who:who + 1]
                cols = slice(t0, t0 + n)
                m = dve.do(V.scalar_tensor_tensor, t[:, cols], xall[:, k, cols],
                           gain[:, k, who:who + 1], rstd[:, cols], ALU.mult, ALU.mult,
                           after=(tg, r, ready))
                a = act.do(S.activation, h_hi[:, k, cols], t[:, cols], ACT.Identity, bias=shift,
                           after=(m, mod_ready[0], *h_readers[0]))
                b = dve.do(V.scalar_tensor_tensor, h_lo[:, k, cols], t[:, cols], shift,
                           f32(h_hi[:, k, cols]), ALU.add, ALU.subtract, after=(a, *h_readers[0]))
            scratch_read[i] = (a, b)
            done += [a, b]
        rstd_readers[0] = gain_readers[0] = (b,)
        return done

    mod_ready, gain_readers, h_readers = [None], [()], [()]

    def adaln(layer, readers):
        stat_w = place(f"cond{layer}", KD * P, F32R, at=arena)
        cond = place(f"cond_silu{layer}", 2 * KD, F32, at=arena + 4 * KD * P)
        row = [place(f"mod_row{layer}_{i}", 512, F32, at=arena + 4 * (KD * P + 16 + 512 * i)) for i in range(2)]
        cw = stat_w.rearrange("p (k m) -> p k m", m=P)
        z = dve.do(V.memset, f32(stat_w), 0.0, after=readers)
        s = act.do(S.activation, cond, param("cond", 0, 2 * KD), ACT.Silu, after=readers)
        c3 = cond.rearrange("p (k w) -> p k w", w=2)
        a = act.do(S.copy, cw[:, :, 0:2], c3, after=(z, s))
        b = dve.do(V.tensor_tensor, cw[:, :, 2:4], c3, f32(cw[:, :, 0:2]), ALU.subtract, after=(a,))
        pe.after(a, b)
        pick = const("pick")
        row_read = [(), ()]
        for chunk in range(12):
            bank, ps = next_banks()
            pe.after(*bank_read[bank])
            for g in range(4):
                hi, lo = weight("mod", layer * 48 + chunk * 4 + g)
                for k in range(2):
                    T.matmul(ps, cw[:, 2 * g + k, :], hi[:, k, :], start=g == 0 and k == 0, stop=False)
                    tok = pe.do(T.matmul, ps, cw[:, 2 * g + k, :], lo[:, k, :], start=False,
                                stop=g == 3 and k == 1)
                done_with_piece(tok)
            r = row[chunk % 2]
            c = act.do(S.copy, r[0:4, :], ps[0:4, :], after=(tok, *row_read[chunk % 2]))
            bank_read[bank] = (c,)
            bank, ps = next_banks()
            pe.after(*bank_read[bank])
            pe.after(c)
            for j in range(4):
                tok = pe.do(T.matmul, ps[:, 2 * j:2 * j + 2], r[0:4, j * P:(j + 1) * P], pick[0:4, :],
                            start=True, stop=True)
            row_read[chunk % 2] = (tok,)
            bias = param("b_mod", layer * 48 + chunk * 4, 4).unsqueeze(2).broadcast_to([P, 4, 2])
            m = dve.do(V.tensor_tensor, mod[:, chunk * 4:chunk * 4 + 4, :],
                       ps[:, 0:8].rearrange("p (c w) -> p c w", w=2), bias, ALU.add,
                       after=(tok, *readers))
            bank_read[bank] = (m,)
        mod_ready[0] = m
        return (tok, m)

    x_ready = [x_in]

    def add_gated(name, idxs, acts, part, segs, after):
        for m, idx in enumerate(idxs):
            bank, ps = next_banks(2)
            pe.after(*bank_read[bank], *bank_read[bank + 1])
            tok = product(name, idx, acts, segs, ps, after=after)
            for who, (t0, n) in enumerate(segs):
                cols = slice(t0, t0 + n)
                d = dve.do(V.scalar_tensor_tensor, xall[:, m, cols], ps[:, cols],
                           mod[:, part * 8 + m, who:who + 1], xall[:, m, cols], ALU.mult, ALU.add,
                           after=(tok, mod_ready[0]))
            bank_read[bank] = bank_read[bank + 1] = (d,)
        x_ready[0] = d
        return tok, d

    def conv3(src, seg_cols, taps, shifts, dst, ready, bias=None):
        lo, hi = seg_cols[0][0], seg_cols[-1][0] + seg_cols[-1][1]
        center = shifts.index(0)
        kw = {"bias": bias} if bias is not None else {}
        last = act.do(S.activation, dst[:, lo:hi], src[:, lo:hi], ACT.Identity, scale=taps[center],
                      after=ready, **kw)
        for tap, shift in zip(taps, shifts):
            if shift == 0:
                continue
            for t0, n in seg_cols:
                to = slice(t0 + max(shift, 0), t0 + n + min(shift, 0))
                of = slice(t0 + max(-shift, 0), t0 + n + min(-shift, 0))
                d = dve.do(V.scalar_tensor_tensor, dst[:, to], src[:, of], tap, dst[:, to],
                           ALU.mult, ALU.add, after=(last, *ready))
            last = d
        return last

    def ffn_half(up, layer, half, segs, acts, h_done, g_hi, g_lo, conv_w, conv_b, shifts, gate_first,
                 func, g_readers):
        width = segs[-1][0] + segs[-1][1]
        for t in range(HALF):
            made = []
            for side in range(2):
                tile = side * FFT + half * HALF + t
                bank, ps = next_banks(2)
                pe.after(*bank_read[bank], *bank_read[bank + 1])
                tok = product(up, layer * 44 + tile, acts, segs, ps, after=h_done)
                i, u = scratch.next()
                act.after(*scratch_read[i])
                dve.after(*scratch_read[i])
                taps = [param(conv_w, (layer * 3 + j) * 44 + tile) for j in range(3)]
                b = param(conv_b, tile) if conv_b else None
                d = conv3(ps, segs, taps, shifts, u, (tok,), bias=b)
                bank_read[bank] = bank_read[bank + 1] = (d,)
                made.append((i, u, d))
            gate, value = (made[0], made[1]) if gate_first else (made[1], made[0])
            s = act.do(S.activation, gate[1][:, 0:width], gate[1][:, 0:width], func, after=(gate[2],))
            m = dve.do(V.tensor_tensor, value[1][:, 0:width], value[1][:, 0:width],
                       gate[1][:, 0:width], ALU.mult, after=(s, value[2]))
            a, b = split_acts(g_hi[:, t, 0:width], g_lo[:, t, 0:width], value[1][:, 0:width],
                              (m, *g_readers))
            scratch_read[gate[0]] = (m,)
            scratch_read[value[0]] = (a, b)
        return (a, b), tok

    def ffn_layer(layer, segs, readers):
        width = segs[-1][0] + segs[-1][1]
        h_done = modulated_norm("norm_ffn", layer, 3, segs, x_ready[0])
        g_hi = tiles(place(f"g_hi{layer}", HALF * width, F32R, at=arena), width)
        g_lo = tiles(place(f"g_lo{layer}", HALF * width, F32R, at=arena + 4 * HALF * width), width)
        for half in range(2):
            g_done, h_used = ffn_half("up", layer, half, segs, (h_hi, h_lo), h_done, g_hi, g_lo,
                                      "conv_ffn", None, [1, 0, -1], False, ACT.Silu, readers)
            tok, _ = add_gated("down", [layer * 16 + half * 8 + m for m in range(KD)], (g_hi, g_lo), 5,
                               segs, g_done)
            readers = (tok,)
        h_readers[0] = (h_used,)
        return (tok, x_ready[0])

    released = adaln(0, ())
    h_done = modulated_norm("norm_mix", 0, 0, SEG_BOTH, x_ready[0])

    PAD = 15
    UW = TALL + 4 * PAD
    CW = UW - 2 * PAD
    ya_hi = tiles(place("ya_hi", 4 * TALL, F32R, at=arena), TALL)
    ya_lo = tiles(place("ya_lo", 4 * TALL, F32R, at=arena + 16 * TALL), TALL)
    upad = tiles(place("upad", 4 * UW, at=arena + 32 * TALL), UW)
    conv = tiles(place("conv", 4 * CW, at=arena + 32 * TALL + 16 * UW), CW)
    yb_hi = tiles(place("yb_hi", 4 * TALL, F32R, at=h_at), TALL)
    yb_lo = tiles(place("yb_lo", 4 * TALL, F32R, at=h_at + 16 * TALL), TALL)
    u_cols = ((0, TX, PAD), (TX, TC, 3 * PAD))
    zeroed = dve.do(V.memset, upad, 0.0, after=released)
    u_done = []
    for t in range(4):
        bank_v, ps_v = next_banks(2)
        pe.after(*bank_read[bank_v], *bank_read[bank_v + 1])
        tok_v = product("in_ab", 12 + t, (h_hi, h_lo), SEG_BOTH, ps_v, after=h_done)
        bank_g, ps_g = next_banks(2)
        pe.after(*bank_read[bank_g], *bank_read[bank_g + 1])
        tok_g = product("in_ab", 16 + t, (h_hi, h_lo), SEG_BOTH, ps_g)
        i, sg = scratch.next()
        act.after(*scratch_read[i])
        a = act.do(S.activation, sg, ps_g[:, 0:TALL], ACT.Sigmoid, after=(tok_g,))
        for t0, n, shift in u_cols:
            d = dve.do(V.tensor_tensor, upad[:, t, t0 + shift:t0 + shift + n], ps_v[:, t0:t0 + n],
                       sg[:, t0:t0 + n], ALU.mult, after=(tok_v, a, zeroed))
        scratch_read[i] = (d,)
        bank_read[bank_v] = bank_read[bank_v + 1] = (d,)
        bank_read[bank_g] = bank_read[bank_g + 1] = (a,)
        u_done.append(d)

    conv_done = {}

    def conv_b_taps():
        for t in range(4):
            w = lambda j: param("conv_b", j * 4 + t)
            d = dve.do(V.tensor_scalar, conv[:, t, :], upad[:, t, 0:CW], w(0), param("conv_b_bias", t),
                       ALU.mult, ALU.add, after=(u_done[t], *released))
            for j in range(1, 31):
                d = dve.do(V.scalar_tensor_tensor, conv[:, t, :], upad[:, t, j:j + CW], w(j),
                           conv[:, t, :], ALU.mult, ALU.add, after=(d,))
                if j % 5 == 0:
                    yield
            conv_done[t] = d
            yield

    taps_left = conv_b_taps()

    def some_taps(n):
        for _ in range(n):
            next(taps_left, None)

    for t in range(4):
        bank_c, ps_c = next_banks(2)
        pe.after(*bank_read[bank_c], *bank_read[bank_c + 1])
        tok_c = product("in_ab", 4 + t, (h_hi, h_lo), SEG_BOTH, ps_c)
        i, gc = scratch.next()
        act.after(*scratch_read[i])
        a = act.do(S.copy, gc, ps_c[:, 0:TALL], after=(tok_c,))
        bank_read[bank_c] = bank_read[bank_c + 1] = (a,)
        some_taps(2)
        bank_u, ps_u = next_banks(2)
        pe.after(*bank_read[bank_u], *bank_read[bank_u + 1])
        tok_u = product("in_ab", 8 + t, (h_hi, h_lo), SEG_BOTH, ps_u)
        d = dve.do(V.tensor_tensor, gc, gc, ps_u[:, 0:TALL], ALU.mult, after=(tok_u, a))
        bank_read[bank_u] = bank_read[bank_u + 1] = (d,)
        some_taps(2)
        j, ca = scratch.next()
        act.after(*scratch_read[j])
        dve.after(*scratch_read[j])
        c = conv3(gc, SEG_BOTH, [param("conv_a", n * 4 + t) for n in range(3)], [1, 0, -1], ca, (d,))
        scratch_read[i] = (c,)
        bank_b, ps_b = next_banks(2)
        pe.after(*bank_read[bank_b], *bank_read[bank_b + 1])
        tok_b = product("in_ab", t, (h_hi, h_lo), SEG_BOTH, ps_b)
        d = dve.do(V.tensor_tensor, ca, ca, ps_b[:, 0:TALL], ALU.mult, after=(tok_b, c))
        bank_read[bank_b] = bank_read[bank_b + 1] = (d,)
        ya = split_acts(ya_hi[:, t, :], ya_lo[:, t, :], ca, (d,))
        scratch_read[j] = (*ya,)
        some_taps(2)
    h_readers[0] = (tok_b,)
    for _ in taps_left:
        pass

    conv_cols = ((0, TX, 0), (TX, TC, 2 * PAD))

    def mean512(src, ready):
        bank, ps = next_banks(2)
        pe.after(*bank_read[bank], *bank_read[bank + 1])
        for t in range(4):
            pe.after(*ready(t))
            for t0, n, shift in conv_cols:
                tok = pe.do(T.matmul, ps[:, t0:t0 + n], mean_ones, src(t)[:, t0 + shift:t0 + shift + n],
                            start=t == 0, stop=t == 3)
        return bank, ps, tok

    bank, ps, tok = mean512(lambda t: conv[:, t, :], lambda t: (conv_done[t],))
    centered = []
    for t in range(4):
        for t0, n, shift in conv_cols:
            c = conv[:, t, t0 + shift:t0 + shift + n]
            d = dve.do(V.scalar_tensor_tensor, c, ps[:, t0:t0 + n], -2.0, c, ALU.mult, ALU.add,
                       after=(tok, conv_done[t]))
        centered.append(d)
    bank_read[bank] = bank_read[bank + 1] = (d,)
    squares = []
    for t in range(4):
        squares.append(act.do(S.activation, upad[:, t, 0:CW], conv[:, t, :], ACT.Square,
                              after=(centered[t], conv_done[t])))
    bank, ps, tok = mean512(lambda t: upad[:, t, :], lambda t: (squares[t],))
    a = act.do(S.activation, rstd, ps[:, 0:TALL], ACT.Sqrt, scale=2.0, bias=param("eps"),
               after=(tok, *rstd_readers[0]))
    bank_read[bank] = bank_read[bank + 1] = (a,)
    r = dve.do(V.reciprocal, rstd, rstd, after=(a,))
    yb = []
    for t in range(4):
        i, s = scratch.next()
        dve.after(*scratch_read[i])
        for t0, n, shift in conv_cols:
            d = dve.do(V.tensor_tensor, s[:, t0:t0 + n], conv[:, t, t0 + shift:t0 + shift + n],
                       rstd[:, t0:t0 + n], ALU.mult, after=(r, centered[t]))
        a = act.do(S.activation, s, s, ACT.Silu, scale=param("ln_g", t), bias=param("ln_b", t), after=(d,))
        yb = split_acts(yb_hi[:, t, :], yb_lo[:, t, :], s, (a, *h_readers[0]))
        scratch_read[i] = (*yb,)
    rstd_readers[0] = (d,)

    class Joined:

        def __init__(self, a, b):
            self.a, self.b = a, b

        def __getitem__(self, key):
            p, k, c = key
            return self.a[p, k, c] if k < 4 else self.b[p, k - 4, c]

    tok, _ = add_gated("out_ab", range(KD), (Joined(ya_hi, yb_hi), Joined(ya_lo, yb_lo)), 2, SEG_BOTH,
                       (*ya, *yb))
    h_readers[0] = (tok,)
    released = ffn_layer(0, SEG_BOTH, (tok, d))

    released = adaln(1, released)
    h_done = modulated_norm("norm_mix", 1, 0, SEG_BOTH, x_ready[0])
    free_at[0] = arena
    qT = tiles(place("qT", 8 * TX), TX)
    kT = tiles(place("kT", 2 * TALL), TALL)
    v_tok = tiles(place("v_tok", 6 * 256), 256)
    rows = [place(f"scores{i}", 4 * 640) for i in range(3)]
    rope_rot = place("rope_rot", P)
    cos_t, sin_t = place("cos", TX), place("sin", TX)
    window = place("window", 384)
    smalls = [place(f"small{i}", 32) for i in range(3)]

    def load_const(dst, name, after):
        at, n = CCOL[name]
        return load(dst, dram["consts"][:, at:at + n], after=after)

    for dst, name in ((rope_rot, "rope_rot"), (cos_t, "cos"), (sin_t, "sin"), (window, "window")):
        c_in = load_const(dst, name, released)
    for e in (pe, act, dve):
        e.after(c_in, *released)

    got = [next_banks() for _ in range(6)]
    for bank, _ in got:
        pe.after(*bank_read[bank])
    tok = product_tokens("v", 0, (h_hi, h_lo), range(6), 256, [ps[:, 0:256] for _, ps in got], after=h_done)
    for b, (bank, ps) in enumerate(got):
        v_ready = act.do(S.copy, v_tok[:, b, :], ps[:, 0:256], after=(tok,))
        bank_read[bank] = (v_ready,)

    def rotary(dst, name, idx, segs, scale):
        bank, ps = next_banks(2)
        pe.after(*bank_read[bank], *bank_read[bank + 1])
        tok = product(name, idx, (h_hi, h_lo), segs, ps)
        i, q = scratch.next()
        act.after(*scratch_read[i])
        a = act.do(S.activation, q[:, 0:TX], ps[:, 0:TX], ACT.Copy, scale=scale, after=(tok,))
        if len(segs) > 1:
            a = act.do(S.copy, dst[:, TX:TALL], ps[:, TX:TALL], after=(tok,))
        bank_read[bank] = bank_read[bank + 1] = (a,)
        bank, ps = next_banks()
        pe.after(*bank_read[bank])
        r = pe.do(T.matmul, ps, rope_rot, q[:, 0:TX], start=True, stop=True, after=(a,))
        j, s = scratch.next()
        dve.after(*scratch_read[j])
        d1 = dve.do(V.tensor_tensor, s[:, 0:TX], ps, sin_t, ALU.mult, after=(r,))
        bank_read[bank] = (d1,)
        d2 = dve.do(V.tensor_tensor, q[:, 0:TX], q[:, 0:TX], cos_t, ALU.mult, after=(a, r))
        d3 = dve.do(V.tensor_tensor, dst[:, 0:TX], q[:, 0:TX], s[:, 0:TX], ALU.add, after=(d1, d2))
        scratch_read[i] = (d3,)
        scratch_read[j] = (d3,)
        return tok, d3, a

    for i in range(2):
        _, k_ready, kc_ready = rotary(kT[:, i, :], "qk", 8 + i, SEG_BOTH, 1.0)
    for i in range(8):
        h_used, q_ready, _ = rotary(qT[:, i, :], "qk", i, SEG_X, HD ** -0.5)
    pe.after(k_ready, kc_ready, q_ready, v_ready)

    O_BANK = 7
    at_hi = tiles(place("at_hi", KD * TX, F32R, at=h_at), TX)
    at_lo = tiles(place("at_lo", KD * TX, F32R, at=h_at + 4 * KD * TX), TX)

    class Unit:
        pass

    def soft(u, gates=None, valid=None, sink=None):
        sm = u.small
        mx, neg, tot, rec, snk = (sm[:, 4 * i:4 * i + 4] for i in range(5))
        d = dve.do(V.tensor_reduce, mx, u.s, AX.X, ALU.max, after=(*u.ready,))
        if sink is not None:
            d = dve.do(V.tensor_tensor, mx, mx, sink, ALU.max, after=(d,))
        n = dve.do(V.tensor_scalar, neg, mx, -1.0, None, ALU.mult, after=(d,))
        if sink is not None:
            k = dve.do(V.tensor_tensor, snk, sink, mx, ALU.subtract, after=(d,))
            ks = act.do(S.activation, snk, snk, ACT.Exp, after=(k,))
        for h in range(4):
            e = act.do(S.activation, u.s[:, h, :], u.s[:, h, :], ACT.Exp, bias=neg[:, h:h + 1],
                       accum_out=tot[:, h:h + 1], after=(n, *u.ready))
        t = e
        if sink is not None:
            t = dve.do(V.tensor_tensor, tot, tot, snk, ALU.add, after=(e, ks))
        r = dve.do(V.reciprocal, rec, tot, after=(t,))
        if gates is not None:
            r = dve.do(V.tensor_tensor, rec, rec, gates, ALU.mult, after=(r,))
        for h in range(4):
            d = dve.do(V.tensor_scalar, u.s[:, h, :], u.s[:, h, :], rec[:, h:h + 1], None, ALU.mult,
                       after=(r, e))
        if valid is not None:
            d = dve.do(V.tensor_tensor, u.s, u.s, valid, ALU.mult, after=(d,))
        u.soft = d

    def apply(u):
        if u.first:
            pe.after(*bank_read[O_BANK])
        o = psum[0:HD, O_BANK * 512:(O_BANK + 1) * 512]
        turned = []

        def turn(c0, n):
            bank, ps = next_banks(among=7)
            pe.after(*bank_read[bank])
            pe.after(u.soft)
            for h in range(4):
                t = pe.do(T.transpose, ps[0:n, h * P:(h + 1) * P], u.s[:, h, c0:c0 + n], ident)
            e = (act, dve)[len(turned) % 2]
            i, pt = scratch.next()
            e.after(*scratch_read[i])
            pt = pt[:, 0:512]
            c = e.do(S.copy if e is act else V.tensor_copy, pt[0:n, :], ps[0:n, :], after=(t,))
            bank_read[bank] = (c,)
            turned.append((i, pt, n, c, t))

        for j, (c0, n, v) in enumerate(u.keys):
            if j == 0:
                turn(c0, n)
            if j + 1 < len(u.keys):
                turn(*u.keys[j + 1][:2])
            i, pt, n, c, _ = turned[j]
            m = pe.do(T.matmul, o, v, pt[0:n, :], start=u.first and j == 0,
                      stop=u.last and j == len(u.keys) - 1, after=(c,))
            scratch_read[i] = (m,)
        u.read = turned[-1][4]
        if u.last:
            dst_hi, dst_lo = u.dst
            src = o.rearrange("p (h q) -> p h q", q=P)
            a = act.do(S.copy, dst_hi, src, after=(m, *u.dst_free))
            b = dve.do(V.tensor_tensor, dst_lo, src, f32(dst_hi), ALU.subtract, after=(a, *u.dst_free))
            bank_read[O_BANK] = (a, b)
            return a, b
        return None

    def run_units(units, scores, softmax):
        done = ()
        for n in range(len(units) + 2):
            if n < len(units):
                units[n].index = n
                units[n].free = (units[n - 3].read,) if n >= 3 else ()
                units[n].small = smalls[n % 3]
                scores(units[n])
            if n >= 2:
                done = apply(units[n - 2]) or done
            if n < len(units):
                softmax(units[n])
        return done

    units = []
    for blk in range(NBLK):
        for g in range(NKV):
            u = Unit()
            u.blk, u.g = blk, g
            u.first = u.last = True
            near = [b for b in (blk - 1, blk, blk + 1) if 0 <= b < NBLK]
            u.near = near
            u.local = len(near) * BLK
            vs = [v_tok[:, b, g * HD:(g + 1) * HD] for b in near + [4, 5]]
            u.keys = [(i * BLK, BLK, v) for i, v in enumerate(vs)]
            half, base = g % 2, 4 * (g // 2)
            rows_ = slice(half * HD, half * HD + HD)
            u.dst = tuple(a[rows_, base:base + 4, blk * BLK:(blk + 1) * BLK] for a in (at_hi, at_lo))
            u.dst_free = (h_used,)
            units.append(u)

    def window_scores(u):
        half, base = u.g % 2, 4 * (u.g // 2)
        on = slice(half * HD, half * HD + HD)
        L = u.local + TC
        u.s = rows[u.index % 3][:, 0:4 * L].rearrange("p (h l) -> p h l", l=L)
        cols = slice(u.near[0] * BLK, (u.near[-1] + 1) * BLK)
        shown = window[:, (u.near[0] - u.blk + 1) * BLK:(u.near[-1] - u.blk + 2) * BLK]
        q = lambda h: qT[on, base + h, u.blk * BLK:(u.blk + 1) * BLK]
        for pair in range(2):
            bank, ps = next_banks(among=7)
            pe.after(*bank_read[bank])
            for h in range(2):
                t = pe.do(T.matmul, ps[:, h * TC:(h + 1) * TC], q(2 * pair + h), kT[on, u.g // 2, TX:TALL],
                          start=True, stop=True)
            a = act.do(S.copy, u.s[:, 2 * pair:2 * pair + 2, u.local:L],
                       ps.rearrange("p (h l) -> p h l", l=TC), after=(t, *u.free))
            bank_read[bank] = (a,)
        for h in range(4):
            bank, ps = next_banks(among=7)
            pe.after(*bank_read[bank])
            t = pe.do(T.matmul, ps[:, 0:u.local], q(h), kT[on, u.g // 2, cols], start=True, stop=True)
            d = dve.do(V.tensor_tensor, u.s[:, h, 0:u.local], ps[:, 0:u.local], shown, ALU.add,
                       after=(t, *u.free))
            bank_read[bank] = (d,)
        u.ready = (a, d)

    def window_softmax(u):
        soft(u, sink=param("sinks", 4 * u.g, 4))

    at_done = run_units(units, window_scores, window_softmax)
    tok, _ = add_gated("o", range(KD), (at_hi, at_lo), 2, SEG_X, at_done)
    h_readers[0] = (tok,)
    released = ffn_layer(1, SEG_X, (tok, *at_done, units[-1].read))

    r = mean_of_squares(lambda k: xall[:, k, 0:TX], KD, SEG_X, lambda k: x_ready[0])
    for k in range(KD):
        d = dve.do(V.scalar_tensor_tensor, xall[:, k, 0:TX], xall[:, k, 0:TX], param("final_norm", k),
                   rstd[:, 0:TX], ALU.mult, ALU.mult, after=(r, x_ready[0]))
    rstd_readers[0] = (d,)
    x_ready[0] = d

    stored = nc.alloc_semaphore("stored_x")
    pool.after(x_ready[0])
    G.dma_start(dram["x_spill"].rearrange("k p t -> p k t"), xall[:, :, 0:TX]).then_inc(stored, 16)
    x_stored = (stored, 16)

    g_hi2 = tiles(place("h2_hi", KD * TX, F32R, at=h_at), TX)
    g_lo2 = tiles(place("h2_lo", KD * TX, F32R, at=h_at + 4 * KD * TX), TX)
    h2 = (g_hi2, g_lo2)

    def plain_norm(src, name, ready, readers):
        r = mean_of_squares(src, KD, SEG_X, lambda k: ready)
        done = []
        for k in range(KD):
            i, t = scratch.next()
            dve.after(*scratch_read[i])
            d = dve.do(V.scalar_tensor_tensor, t[:, 0:TX], src(k), param(name, k), rstd[:, 0:TX],
                       ALU.mult, ALU.mult, after=(r, ready))
            ab = split_acts(g_hi2[:, k, :], g_lo2[:, k, :], t[:, 0:TX], (d, *readers))
            scratch_read[i] = (*ab,)
            done += ab
        rstd_readers[0] = (d,)
        return done

    h_done = plain_norm(lambda k: xall[:, k, 0:TX], "pre_mix", x_ready[0], released)

    arena2 = h_at + 8 * KD * TX
    free_at[0] = arena2
    ssm_hi = tiles(place("ssm_hi", KD * TX, F32R), TX)
    ssm_lo = tiles(place("ssm_lo", KD * TX, F32R), TX)
    branch_at = free_at[0]

    x_tok = tiles(place("x_tok", NBLK * D), D)
    z_tok = tiles(place("z_tok", NBLK * D, at=x_at), D)
    b_tok = tiles(place("b_tok", NBLK * 512), 512)
    bT = tiles(place("bT", 4 * TX), TX)
    cT = tiles(place("cT", 4 * TX, at=x_at + 4 * NBLK * D), TX)
    x_dt = place("x_dt", D)
    x_end = place("x_end", D)
    state = tiles(place("state", SSM_G * 256), 256)
    ch = place("carried", D)
    dt_t = ssm_small[:, 0:64].rearrange("p (c h) -> p c h", h=16)
    dta = ssm_small[:, 64:128].rearrange("p (c h) -> p c h", h=16)
    tmp64 = ssm_small[:, 128:192].rearrange("p (c h) -> p c h", h=16)
    a_neg = ssm_small[:, 192:208]
    e_acum = ssm_small[:, 208:224]
    to_end = ssm_small[:, 224:240]
    e_last = ssm_small[:, 240:256]
    gates = ssm_small[:, 256:352].rearrange("p (c h) -> p c h", h=24)
    gsum = ssm_small[:, 352:356]
    grec = ssm_small[:, 356:360]

    got = [next_banks() for _ in range(4)]
    for bank, _ in got:
        pe.after(*bank_read[bank])
    tok = product_tokens("dtg", 0, h2, range(4), 40, [ps[:, 0:40] for _, ps in got], after=h_done)
    for c, (bank, ps) in enumerate(got):
        d = dve.do(V.tensor_tensor, dt_t[:, c, :], ps[:, 0:16], param("dt_bias", 0, 16), ALU.add,
                   after=(tok, *released))
        a_g = act.do(S.activation, gates[:, c, :], ps[:, 16:40], ACT.Sigmoid, after=(tok, d, *released))
        bank_read[bank] = (d, a_g)
    d1 = dve.do(V.tensor_scalar, tmp64, dt_t, -1.0, None, ALU.mult, after=(d,))
    d1 = dve.do(V.tensor_tensor, tmp64, tmp64, dt_t, ALU.min, after=(d1,))
    a = act.do(S.activation, tmp64, tmp64, ACT.Exp, after=(d1,))
    a = act.do(S.activation, tmp64, tmp64, ACT.Ln, bias=1.0, after=(a,))
    d = dve.do(V.scalar_tensor_tensor, dt_t, dt_t, 0.0, tmp64, ALU.max, ALU.add, after=(a,))
    a = act.do(S.activation, a_neg, param("a_log", 0, 16), ACT.Exp, after=released)
    d1 = dve.do(V.tensor_scalar, a_neg, a_neg, -1.0, None, ALU.mult, after=(a,))
    dt_ready = dve.do(V.tensor_tensor, dta, dt_t, a_neg.unsqueeze(1).broadcast_to([P, 4, 16]), ALU.mult,
                      after=(d, d1))

    pending = None

    def turn_tile(src, ready, dst, free_slot):
        bank, ps = next_banks()
        pe.after(*bank_read[bank])
        for c in range(4):
            t = pe.do(T.transpose, ps[:, c * P:(c + 1) * P], src[:, c * P:(c + 1) * P], ident,
                      after=(ready,))
        a = act.do(S.copy, dst, ps.rearrange("p (c f) -> p c f", f=P), after=(t, *released))
        bank_read[bank] = (a,)
        if free_slot is not None:
            scratch_read[free_slot] = (t,)
        return a

    for m in range(16):
        bank, ps = next_banks(2)
        pe.after(*bank_read[bank], *bank_read[bank + 1])
        tok = product("xbc", m, h2, SEG_X, ps)
        if pending:
            xb_ready = turn_tile(*pending)
            pending = None
        i, u = scratch.next()
        act.after(*scratch_read[i])
        dve.after(*scratch_read[i])
        taps = [param("ssm_conv_w", j * 16 + m) for j in range(4)]
        d = conv3(ps, SEG_X, taps, [3, 2, 1, 0], u, (tok,), bias=param("ssm_conv_b", m))
        bank_read[bank] = bank_read[bank + 1] = (d,)
        if m < 8:
            a = act.do(S.activation, u[:, 0:TX], u[:, 0:TX], ACT.Silu, after=(d,))
            pending = (u, a, x_tok[:, :, m * P:(m + 1) * P], i)
        elif m < 12:
            a = act.do(S.activation, bT[:, m - 8, :], u[:, 0:TX], ACT.Silu, after=(d, *released))
            scratch_read[i] = (a,)
            pending = (bT[:, m - 8, :], a, b_tok[:, :, (m - 8) * P:(m - 7) * P], None)
        else:
            a = act.do(S.activation, cT[:, m - 12, :], u[:, 0:TX], ACT.Silu, after=(d, x_stored))
            scratch_read[i] = (a,)
    c_ready = a
    bt_ready = a

    for half in range(2):
        got = [next_banks() for _ in range(4)]
        for bank, _ in got:
            pe.after(*bank_read[bank])
        tok = product_tokens("z", half * 4, h2, range(4), 512, [ps for _, ps in got])
        for c, (bank, ps) in enumerate(got):
            z_ready = act.do(S.activation, z_tok[:, c, half * 512:(half + 1) * 512], ps, ACT.Silu,
                             after=(tok, x_stored))
            bank_read[bank] = (z_ready,)
    pe.after(xb_ready, dt_ready, c_ready, z_ready)
    dve.after(xb_ready, dt_ready, c_ready, z_ready)

    def heads(ap, width=SSM_P):
        return ap.rearrange("p (h w) -> p h w", w=width)

    def per_head(ap, width=SSM_P):
        n = ap.shape[1]
        return ap.unsqueeze(2).broadcast_to([P, n, width])

    turned_done = ()
    ch_read = ()
    xe_read = ()
    xdt_read = ()
    st_ready = None
    for c in range(NBLK):
        tokens = slice(c * BLK, (c + 1) * BLK)
        bank, ps = next_banks()
        pe.after(*bank_read[bank])
        t = pe.do(T.matmul, ps[:, 0:16], const("upto"), dta[:, c, :], start=True, stop=True)
        a = act.do(S.activation, e_acum, ps[:, 0:16], ACT.Exp, after=(t, *ch_read))
        bank_read[bank] = (a,)
        ea_ready = a
        dx = dve.do(V.tensor_tensor, heads(x_dt), heads(x_tok[:, c, :]), per_head(dt_t[:, c, :]), ALU.mult,
                    after=(*xdt_read,))
        if c < NBLK - 1:
            bank, ps = next_banks()
            pe.after(*bank_read[bank])
            t = pe.do(T.matmul, ps[:, 0:16], const("later"), dta[:, c, :], start=True, stop=True)
            a1 = act.do(S.activation, to_end, ps[:, 0:16], ACT.Exp, after=(t, *xe_read))
            bank_read[bank] = (a1,)
            bank, ps = next_banks()
            pe.after(*bank_read[bank])
            t = pe.do(T.matmul, ps[:, 0:16], mean_ones, dta[:, c, :], start=True, stop=True)
            a2 = act.do(S.activation, e_last, ps[:, 0:16], ACT.Exp, scale=float(D), after=(t, *xe_read))
            bank_read[bank] = (a2,)
            xe_ready = dve.do(V.tensor_tensor, heads(x_end), heads(x_dt), per_head(to_end), ALU.mult,
                              after=(a1, dx, *xe_read))
        pe.after(*bank_read[6], *bank_read[7])
        ps_y = bank_cols(6, 2)
        pre = {}

        def prepare(g):
            i, steps = scratch.next()
            dve.after(*scratch_read[i])
            d = dve.do(V.tensor_tensor, heads(steps[:, 0:512], P),
                       const("upto").unsqueeze(1).broadcast_to([P, 4, P]),
                       per_head(dta[:, c, 4 * g:4 * g + 4], P), ALU.mult)
            bank, ps = next_banks(among=6)
            pe.after(*bank_read[bank])
            t = pe.do(T.matmul, ps, const("later"), steps[:, 0:512], start=True, stop=True, after=(d,))
            j, decay = scratch.next()
            act.after(*scratch_read[j])
            a = act.do(S.activation, decay[:, 0:512], ps, ACT.Exp, after=(t,))
            bank_read[bank] = (a,)
            scratch_read[i] = (t,)
            bank, ps = next_banks(among=6)
            pe.after(*bank_read[bank])
            t = pe.do(T.matmul, ps[:, 0:P], bT[:, g, tokens], cT[:, g, tokens], start=True, stop=True)
            k, cb = scratch.next()
            dve.after(*scratch_read[k])
            d = dve.do(V.tensor_tensor, cb[:, 0:P], ps[:, 0:P], const("upto"), ALU.mult, after=(t,))
            bank_read[bank] = (d,)
            d = dve.do(V.tensor_tensor, heads(decay[:, 0:512], P), heads(decay[:, 0:512], P),
                       cb[:, 0:P].unsqueeze(1).broadcast_to([P, 4, P]), ALU.mult, after=(a, d))
            scratch_read[k] = (d,)
            pre[g] = (j, decay, d)

        prepare(0)
        for g in range(SSM_G):
            if g + 1 < SSM_G:
                prepare(g + 1)
            j, w, ready = pre[g]
            pe.after(ready, dx)
            for h in range(4):
                col = (4 * g + h) * SSM_P
                t_y = pe.do(T.matmul, ps_y[:, col:col + SSM_P], w[:, h * P:(h + 1) * P],
                            x_dt[:, col:col + SSM_P], start=True, stop=True)
            scratch_read[j] = (t_y,)
        y = z_tok[:, c, :]
        ch_ready = []
        if c > 0:
            for half in range(2):
                bank, ps = next_banks(among=6)
                pe.after(*bank_read[bank])
                for g2 in range(2):
                    g = 2 * half + g2
                    t = pe.do(T.matmul, ps[:, g2 * 256:(g2 + 1) * 256], cT[:, g, tokens], state[:, g, :],
                              start=True, stop=True, after=(st_ready,))
                cols = slice(half * 512, (half + 1) * 512)
                d = dve.do(V.tensor_tensor, heads(ch[:, cols]), heads(ps),
                           per_head(e_acum[:, 8 * half:8 * half + 8]), ALU.mult, after=(t, ea_ready))
                bank_read[bank] = (d,)
                ch_ready.append(d)
            st_read = t
        if c < NBLK - 1:
            for half in range(2):
                bank, ps = next_banks(among=6)
                pe.after(*bank_read[bank])
                for g2 in range(2):
                    g = 2 * half + g2
                    t = pe.do(T.matmul, ps[:, g2 * 256:(g2 + 1) * 256], b_tok[:, c, g * P:(g + 1) * P],
                              x_end[:, g * 256:(g + 1) * 256], start=True, stop=True, after=(xe_ready,))
                st = state[:, 2 * half:2 * half + 2, :].rearrange("p g c -> p (g c)")
                if c == 0:
                    d = dve.do(V.tensor_copy, st, ps, after=(t, *released))
                else:
                    d = dve.do(V.tensor_tensor, heads(st), heads(st), per_head(e_last[:, 8 * half:8 * half + 8]),
                               ALU.mult, after=(a2, st_read))
                    d = dve.do(V.tensor_tensor, st, st, ps, ALU.add, after=(d, t))
                bank_read[bank] = (d,)
            st_ready = d
            xe_read = (t, d)
        i0, s0 = scratch.next()
        dve.after(*scratch_read[i0])
        i1, s1 = scratch.next()
        dve.after(*scratch_read[i1])
        for half, s in enumerate((s0, s1)):
            cols = slice(half * 512, (half + 1) * 512)
            s = s[:, 0:512]
            d = dve.do(V.tensor_tensor, heads(s), heads(x_tok[:, c, cols]),
                       per_head(param("ssm_d", 8 * half, 8)), ALU.mult)
            d = dve.do(V.tensor_tensor, s, s, ps_y[:, cols], ALU.add, after=(d, t_y))
            if c > 0:
                d = dve.do(V.tensor_tensor, s, s, ch[:, cols], ALU.add, after=(d, ch_ready[half]))
            d = dve.do(V.tensor_tensor, y[:, cols], y[:, cols], s, ALU.mult, after=(d,))
        bank_read[6] = bank_read[7] = (d,)
        scratch_read[i0] = (d,)
        scratch_read[i1] = (d,)
        ch_read = (d,)
        xdt_read = (t_y, d) if c == NBLK - 1 else (t_y, xe_ready)
        i, sq = scratch.next()
        act.after(*scratch_read[i])
        a = None
        for g in range(SSM_G):
            a = act.do(S.activation, sq[:, 0:256], y[:, g * 256:(g + 1) * 256], ACT.Square,
                       accum_out=gsum[:, g:g + 1], after=(a, d, *turned_done))
        scratch_read[i] = (a,)
        a = act.do(S.activation, gsum, gsum, ACT.Sqrt, scale=1.0 / 256, bias=param("eps"), after=(a,))
        r = dve.do(V.reciprocal, grec, gsum, after=(a,))
        for g in range(SSM_G):
            d = dve.do(V.tensor_scalar, y[:, g * 256:(g + 1) * 256], y[:, g * 256:(g + 1) * 256],
                       grec[:, g:g + 1], None, ALU.mult, after=(r, d))
        for half in range(2):
            bank, ps = next_banks(among=6)
            pe.after(*bank_read[bank])
            for j in range(4):
                t = pe.do(T.transpose, ps[:, j * P:(j + 1) * P],
                          y[:, (4 * half + j) * P:(4 * half + j + 1) * P], ident, after=(d,))
            gain_b = param("ssm_norm", 4 * half, 4).unsqueeze(2).broadcast_to([P, 4, P])
            i, s = scratch.next()
            dve.after(*scratch_read[i])
            s3 = heads(s[:, 0:512], P)
            m = dve.do(V.tensor_tensor, s3, heads(ps, P), gain_b, ALU.mult, after=(t,))
            bank_read[bank] = (m,)
            ssm_done = split_acts(ssm_hi[:, 4 * half:4 * half + 4, tokens],
                                  ssm_lo[:, 4 * half:4 * half + 4, tokens], s3, (m, *released))
            scratch_read[i] = (*ssm_done,)
        turned_done = (t, d)

    released = (*ssm_done, t, d, t_y)

    free_at[0] = branch_at
    sb_hi = tiles(place("sb_hi", SB_H * TX, F32R), TX)
    sb_lo = tiles(place("sb_lo", SB_H * TX, F32R), TX)
    nsa_hi = tiles(place("nsa_hi", 4 * TX, F32R), TX)
    nsa_lo = tiles(place("nsa_lo", 4 * TX, F32R, at=x_at + 4 * KD * TX), TX)
    nsa_at = free_at[0]
    sb_qT = tiles(place("sb_qT", SB_H * TX), TX)
    sb_kT = tiles(place("sb_kT", SB_H * TX), TX)
    sb_v = tiles(place("sb_v", NBLK * 512, at=x_at), 512)
    sp = tiles(place("softplus_z", NBLK * TX), TX)
    wgt = tiles(place("sb_w", NBLK * TX, at=x_at + 4 * NBLK * 512), TX)
    for m in range(8):
        bank, ps = next_banks()
        pe.after(*bank_read[bank])
        tok = product("sbqk", m, h2, SEG_X, ps)
        dst = (sb_qT if m < 4 else sb_kT)[:, m % 4, :]
        a = act.do(S.activation, dst, ps, ACT.Copy, scale=128 ** -0.5 if m < 4 else 1.0,
                   after=(tok, *released))
        bank_read[bank] = (a,)
    qk_ready = a
    got = [next_banks() for _ in range(4)]
    for bank, _ in got:
        pe.after(*bank_read[bank])
    tok = product_tokens("sbv", 0, h2, range(4), 512, [ps for _, ps in got])
    for c, (bank, ps) in enumerate(got):
        a = act.do(S.copy, sb_v[:, c, :], ps, after=(tok, *released))
        bank_read[bank] = (a,)
    pe.after(qk_ready, a)
    dve.after(*released)
    act.after(*released)
    w_read = ()
    for h in range(SB_H):
        held = []
        for kb in range(NBLK):
            n = TX - kb * BLK
            bank, ps = next_banks(among=7)
            pe.after(*bank_read[bank])
            t = pe.do(T.matmul, ps[:, 0:n], sb_kT[:, h, kb * BLK:(kb + 1) * BLK],
                      sb_qT[:, h, kb * BLK:TX], start=True, stop=True)
            s = sp[:, kb, 0:n]
            i, e = scratch.next()
            dve.after(*scratch_read[i])
            e = e[:, 0:n]
            d = dve.do(V.tensor_scalar, e, ps[:, 0:n], -1.0, None, ALU.mult, after=(t,))
            d = dve.do(V.tensor_tensor, e, ps[:, 0:n], e, ALU.min, after=(d,))
            a = act.do(S.activation, e, e, ACT.Exp, after=(d,))
            a = act.do(S.activation, e, e, ACT.Ln, bias=1.0, after=(a,))
            d = dve.do(V.scalar_tensor_tensor, s, ps[:, 0:n], 0.0, e, ALU.max, ALU.add,
                       after=(a, *w_read))
            scratch_read[i] = (d,)
            d = dve.do(V.tensor_tensor, s[:, 0:BLK], s[:, 0:BLK], const("before"), ALU.mult, after=(d,))
            held.append((bank, ps, d))
        for kb in range(NBLK - 1, -1, -1):
            bank, ps, _ = held[kb]
            for kb2 in range(kb, NBLK):
                q0 = (kb2 - kb) * BLK
                t = pe.do(T.matmul, ps[:, q0:TX - kb * BLK], const("neg_from" if kb2 == kb else "neg_one"),
                          sp[:, kb2, 0:TX - kb2 * BLK], start=False, stop=kb2 == NBLK - 1,
                          skip_group_check=True, after=(*(x[2] for x in held),))
            n = TX - kb * BLK
            a = act.do(S.activation, wgt[:, kb, 0:n], ps[:, 0:n], ACT.Exp, after=(t, *w_read))
            bank_read[bank] = (a,)
            d = dve.do(V.tensor_tensor, wgt[:, kb, 0:BLK], wgt[:, kb, 0:BLK], const("before"), ALU.mult,
                       after=(a,))
        sp_read = t
        bank, ps = 7, bank_cols(7)
        pe.after(*bank_read[7])
        for kb in range(NBLK):
            t = pe.do(T.matmul, ps[:, kb * BLK:TX], sb_v[:, kb, h * P:(h + 1) * P],
                      wgt[:, kb, 0:TX - kb * BLK], start=kb == 0, stop=kb == NBLK - 1, after=(a, d))
        w_read = (sp_read, t)
        sb_done = split_acts(sb_hi[:, h, :], sb_lo[:, h, :], ps, (t, *released))
        bank_read[bank] = (*sb_done,)
    released = (*sb_done, t)

    free_at[0] = nsa_at
    nq = tiles(place("nq", 4 * TX), TX)
    nk = tiles(place("nk", 2 * TX), TX)
    nv = tiles(place("nv", NBLK * 256), 256)
    dist = place("dist", 512)
    kc = place("kc", 32)
    vc = place("vc", P)
    nsa_rows = place("nsa_scores0", 2048), place("nsa_scores1", 2048, at=x_at), \
        place("nsa_scores2", 2048, at=x_at + 8192)
    smalls = [place(f"nsmall{i}", 32) for i in range(3)]
    late_at = free_at[0]
    cd_t = place("cmp_dist", 4 * NCMP).rearrange("p (b n) -> p b n", n=NCMP)
    cv_t = place("cmp_valid", 4 * NCMP).rearrange("p (b n) -> p b n", n=NCMP)
    w1 = place("cmp_w1", CMP_LEN * P, at=x_at).rearrange("p (l o) -> p l o", o=P)
    w2 = place("cmp_w2", P, at=late_at)
    pos = place("cmp_pos", CMP_LEN, at=late_at + 512)
    for dst, name in ((dist, "dist"),):
        c_in = load_const(dst, name, released)

    gates_ready = a_g
    hid_ready = None
    pos_blocks = tiles(nq.rearrange("p k t -> p (k t)")[:, 0:CMP_LEN * NCMP], NCMP)
    hid = nsa_rows[0][:, 0:32]
    w_used = released
    for which in range(2):
        w1_in = load(w1, dram[f"cmp_w1_{which}"], after=(*w_used,))
        w2_in = load(w2, dram[f"cmp_w2_{which}"], after=(*w_used,))
        pos_in = load(pos, dram[f"cmp_pos_{which}"], after=(*w_used,))
        bank, ps = next_banks()
        pe.after(*bank_read[bank])
        tok = product("nk", which, h2, SEG_X, ps)
        i, s = scratch.next()
        act.after(*scratch_read[i])
        a = act.do(S.copy, s[:, 0:TX], ps, after=(tok,))
        bank_read[bank] = (a,)
        for lh in range(2):
            src = s[:, lh * 16:lh * 16 + NCMP * 16].rearrange("p (n l) -> p l n", l=16)
            d = dve.do(V.tensor_tensor, pos_blocks[:, lh * 16:lh * 16 + 16, :], src,
                       pos[:, lh * 16:lh * 16 + 16].unsqueeze(2).broadcast_to([P, 16, NCMP]), ALU.add,
                       after=(a, pos_in, *w_used))
        scratch_read[i] = (d,)
        bank, ps = next_banks()
        pe.after(*bank_read[bank])
        pe.after(d, w1_in, w2_in)
        for l in range(CMP_LEN):
            t = pe.do(T.matmul, ps[:, 0:NCMP], w1[:, l, :], pos_blocks[:, l, :], start=l == 0,
                      stop=l == CMP_LEN - 1)
        a = act.do(S.activation, hid[:, 0:NCMP], ps[:, 0:NCMP], ACT.Silu, after=(t, *w_used))
        bank_read[bank] = (a,)
        bank, ps = next_banks()
        pe.after(*bank_read[bank])
        if which == 0:
            t = pe.do(T.matmul, ps[:, 0:NCMP], w2, hid[:, 0:NCMP], start=True, stop=True, after=(a,))
            a = kc_ready = act.do(S.copy, kc[:, 0:NCMP], ps[:, 0:NCMP], after=(t, *released))
        else:
            t = pe.do(T.matmul, ps[0:NCMP, 0:P], hid[:, 0:NCMP], w2, start=True, stop=True, after=(a,))
            a = vc_ready = act.do(S.copy, vc[0:NCMP, :], ps[0:NCMP, 0:P], after=(t, *released))
        bank_read[bank] = (a,)
        w_used = (t, a, d)
    for dst, name in ((cd_t.rearrange("p b n -> p (b n)"), "cmp_dist"),
                      (cv_t.rearrange("p b n -> p (b n)"), "cmp_valid")):
        c_in = load_const(dst, name, w_used)
    for m in (2, 3):
        bank, ps = next_banks()
        pe.after(*bank_read[bank])
        tok = product("nk", m, h2, SEG_X, ps)
        a = act.do(S.copy, nk[:, m - 2, :], ps, after=(tok, *released))
        bank_read[bank] = (a,)
    got = [next_banks() for _ in range(4)]
    for bank, _ in got:
        pe.after(*bank_read[bank])
    tok = product_tokens("nv", 0, h2, range(4), 256, [ps[:, 0:256] for _, ps in got])
    for c, (bank, ps) in enumerate(got):
        a = act.do(S.copy, nv[:, c, :], ps[:, 0:256], after=(tok, *released))
        bank_read[bank] = (a,)
    for m in range(4):
        bank, ps = next_banks()
        pe.after(*bank_read[bank])
        tok = product("nq", m, h2, SEG_X, ps)
        a = act.do(S.activation, nq[:, m, :], ps, ACT.Copy, scale=HD ** -0.5, after=(tok, *w_used))
        bank_read[bank] = (a,)
    for e in (pe, dve, act):
        e.after(a, c_in, kc_ready, vc_ready, gates_ready, *w_used)

    units = []
    for blk in range(NBLK):
        for g in range(NSA_G):
            for branch in range(3):
                u = Unit()
                u.blk, u.g, u.branch = blk, g, branch
                u.first, u.last = branch == 0, branch == 2
                if branch == 0:
                    u.keys = [(0, NCMP, vc[0:NCMP, g * HD:(g + 1) * HD])]
                else:
                    v0 = (branch - 1) * P + g * HD
                    u.keys = [(b * BLK, BLK, nv[:, b, v0:v0 + HD]) for b in range(blk + 1)]
                u.dst = tuple(a_[g * HD:(g + 1) * HD, :, blk * BLK:(blk + 1) * BLK]
                              for a_ in (nsa_hi, nsa_lo))
                u.dst_free = released
                units.append(u)

    def sparse_scores(u):
        on = slice(u.g * HD, (u.g + 1) * HD)
        q = lambda h: nq[on, h, u.blk * BLK:(u.blk + 1) * BLK]
        buf = nsa_rows[u.index % 3]
        if u.branch == 0:
            u.s = buf[:, 0:4 * NCMP].rearrange("p (h l) -> p h l", l=NCMP)
            bank, ps = next_banks(among=7)
            pe.after(*bank_read[bank])
            for h in range(4):
                t = pe.do(T.matmul, ps[:, h * NCMP:(h + 1) * NCMP], q(h), kc[on, 0:NCMP],
                          start=True, stop=True)
            for h in range(4):
                d = dve.do(V.scalar_tensor_tensor, u.s[:, h, :], cd_t[:, u.blk, :], SLOPES[4 * u.g + h],
                           ps[:, h * NCMP:(h + 1) * NCMP], ALU.mult, ALU.add, after=(t, *u.free))
            bank_read[bank] = (d,)
            u.ready = (d,)
            return
        L = (u.blk + 1) * BLK
        u.s = buf[:, 0:4 * L].rearrange("p (h l) -> p h l", l=L)
        for h in range(4):
            bank, ps = next_banks(among=7)
            pe.after(*bank_read[bank])
            t = pe.do(T.matmul, ps[:, 0:L], q(h), nk[on, u.branch - 1, 0:L], start=True, stop=True)
            d = dve.do(V.scalar_tensor_tensor, u.s[:, h, :], dist[:, TX - L:TX], SLOPES[4 * u.g + h],
                       ps[:, 0:L], ALU.mult, ALU.add, after=(t, *u.free))
            bank_read[bank] = (d,)
        u.ready = (d,)

    def sparse_softmax(u):
        g0 = u.branch * NSA_H + 4 * u.g
        valid = None
        if u.branch == 0:
            valid = cv_t[:, u.blk, :].unsqueeze(1).broadcast_to([P, 4, NCMP])
        soft(u, gates=gates[:, u.blk, g0:g0 + 4], valid=valid)

    nsa_done = run_units(units, sparse_scores, sparse_softmax)
    released = (*nsa_done, units[-1].read, units[-2].read)

    mix_hi = tiles(place("mix_hi", KD * TX, F32R, at=x_at), TX)
    mix_lo = tiles(place("mix_lo", KD * TX, F32R, at=nsa_at), TX)
    branches = (("br_ssm", (ssm_hi, ssm_lo), ssm_done), ("br_sb", (sb_hi, sb_lo), sb_done),
                ("br_nsa", (nsa_hi, nsa_lo), nsa_done))
    for m in range(KD):
        i, total = scratch.next()
        dve.after(*scratch_read[i])
        for n, (name, ys, ready) in enumerate(branches):
            bank_g, ps_g = next_banks()
            pe.after(*bank_read[bank_g])
            tok = product("gate", 8 * n + m, h2, SEG_X, ps_g)
            j, sg = scratch.next()
            act.after(*scratch_read[j])
            a = act.do(S.activation, sg[:, 0:TX], ps_g, ACT.Sigmoid, after=(tok,))
            bank_read[bank_g] = (a,)
            bank, ps = next_banks()
            pe.after(*bank_read[bank])
            tok = product(name, m, ys, SEG_X, ps, after=ready)
            dst = total if n == 0 else sg
            d = dve.do(V.tensor_tensor, dst[:, 0:TX], sg[:, 0:TX], ps, ALU.mult, after=(a, tok))
            bank_read[bank] = (d,)
            if n:
                d = dve.do(V.tensor_tensor, total[:, 0:TX], total[:, 0:TX], sg[:, 0:TX], ALU.add, after=(d,))
            scratch_read[j] = (d,)
        mix_done = split_acts(mix_hi[:, m, :], mix_lo[:, m, :], total[:, 0:TX], (d, *released))
        scratch_read[i] = (*mix_done,)
    h_used = tok

    x2 = tiles(place("x2", KD * TX, at=arena2), TX)
    y2 = tiles(place("y2", KD * TX, at=arena2 + 4 * KD * TX), TX)
    x_in = load(x2, dram["x_spill"].rearrange("k p t -> p k t"), after=(x_stored, tok))

    y_done = []
    for m in range(KD):
        bank, ps = next_banks()
        pe.after(*bank_read[bank])
        tok = product("out2", m, (mix_hi, mix_lo), SEG_X, ps, after=mix_done)
        a = act.do(S.copy, y2[:, m, :], ps, after=(tok, h_used))
        bank_read[bank] = (a,)
        y_done.append(a)

    def add_normed(name):
        r = mean_of_squares(lambda k: y2[:, k, :], KD, SEG_X, lambda k: y_done[k])
        for k in range(KD):
            i, t = scratch.next()
            dve.after(*scratch_read[i])
            d = dve.do(V.scalar_tensor_tensor, t[:, 0:TX], y2[:, k, :], param(name, k), rstd[:, 0:TX],
                       ALU.mult, ALU.mult, after=(r,))
            d = dve.do(V.tensor_tensor, x2[:, k, :], x2[:, k, :], t[:, 0:TX], ALU.add, after=(d, x_in))
            scratch_read[i] = (d,)
        rstd_readers[0] = (d,)
        return d

    x_ready[0] = add_normed("post_mix")
    y_free = x_ready[0]
    h_done = plain_norm(lambda k: x2[:, k, :], "pre_ffn", x_ready[0], (h_used,))

    ff_at = arena2 + 8 * KD * TX
    g_hi = tiles(place("g2_hi", HALF * TX, F32R, at=x_at), TX)
    g_lo = tiles(place("g2_lo", HALF * TX, F32R, at=ff_at), TX)
    readers = (tok,)
    for half in range(2):
        g_done, _ = ffn_half("up2", 0, half, SEG_X, h2, h_done, g_hi, g_lo, "conv_ffn2", "conv_ffn2_b",
                             [2, 1, 0], True, ACT.Gelu_apprx_tanh, readers)
        for m in range(KD):
            bank, ps = next_banks()
            pe.after(*bank_read[bank])
            tok = product("down2", half * 8 + m, (g_hi, g_lo), SEG_X, ps, after=g_done)
            if half == 0:
                a = act.do(S.copy, y2[:, m, :], ps, after=(tok, y_free))
            else:
                a = dve.do(V.tensor_tensor, y2[:, m, :], y2[:, m, :], ps, ALU.add, after=(tok, y_done[m]))
            bank_read[bank] = (a,)
            y_done[m] = a
        readers = (tok,)
    last = add_normed("post_ffn")

    pool.after(last)
    G.dma_start(out.rearrange("k p t -> p k t"), x2).then_inc(stored, 16)
    pool.after((stored, 32))

    assert next_piece[0] == len(plan)
    sp_q = Engine(nc, nc.sync, "sp")
    for i, (name, idx) in enumerate(plan):
        _, kt, n = WEIGHTS[name]
        if i >= NRAW:
            sp_q.after(*raw_read[i - NRAW])
        nc.sync.dma_start(raw[i % NRAW][:, 0:kt * n], dram[name][idx]).then_inc(raw_sem[i % NRAW], 16)


def by_feature(w):
    k, m = w.shape
    return w.reshape(k // P, P, m // P, P).transpose(2, 1, 0, 3).reshape(m // P, P, -1)


def by_rows(w, kt, n):
    k, m = w.shape
    return w.reshape(k // P // kt, kt, P, m // n, n).transpose(3, 0, 2, 1, 4).reshape(-1, P, kt * n)


def column(v):
    return np.ascontiguousarray(v.reshape(-1, P).T)


def head_order(per_tile):
    return np.concatenate([np.arange(h * HD, (h + 1) * HD) for h in per_tile])


Q_ORDER = head_order([8 * (i // 4) + i % 4 + 4 * s for i in range(8) for s in range(2)])
NQ_ORDER = head_order([i + 4 * s for i in range(4) for s in range(2)])


def constants():
    r = np.arange(P)
    c = {
        "ident": np.eye(P), "upto": r[:, None] <= r[None, :], "later": r[:, None] > r[None, :],
        "neg_from": -1.0 * (r[:, None] >= r[None, :]),
        "neg_one": -np.ones((P, P)), "before": r[:, None] < r[None, :],
    }
    pick = np.zeros((P, 2))
    pick[[0, 2], 0] = 1
    pick[[1, 3], 1] = 1
    c["pick"] = pick
    rot = np.zeros((P, P))
    half = HD // 2
    for base in (0, HD):
        for i in range(half):
            rot[base + half + i, base + i] = -1.0
            rot[base + i, base + half + i] = 1.0
    c["rope_rot"] = rot
    n_freq = HD // 4
    inv = np.float32(10000.0) ** (-np.arange(n_freq, dtype=np.float32) / np.float32(n_freq))
    t = np.arange(TX)
    ang = np.concatenate([(t // GRID_W).astype(np.float32)[:, None] * inv,
                          (t % GRID_W).astype(np.float32)[:, None] * inv], axis=-1).T
    c["cos"] = np.tile(np.cos(ang), (4, 1))
    c["sin"] = np.tile(np.sin(ang), (4, 1))
    w = np.zeros((P, 384))
    w[:, 0:128][r[None, :] < r[:, None]] = NEG
    w[:, 256:384][r[None, :] > r[:, None]] = NEG
    c["window"] = w
    d = (r[:, None] + 384) - np.arange(512)[None, :]
    c["dist"] = np.where(d >= 0, -1.0 * d, NEG)
    q = np.arange(TX).reshape(NBLK, P)
    end = np.arange(NCMP) * CMP_STRIDE + CMP_LEN - 1
    dc = q[:, :, None] - end[None, None, :]
    c["cmp_dist"] = np.where(dc >= 0, -1.0 * dc, NEG).transpose(1, 0, 2).reshape(P, -1)
    c["cmp_valid"] = (dc >= 0).transpose(1, 0, 2).reshape(P, -1)
    return np.concatenate([np.asarray(c[n], np.float32) for n, _ in CONST_COLS], axis=1)


def kernel(**inputs):
    from concourse import bacc
    from concourse.bass_utils import run_bass_kernel_spmd

    a = {k: np.asarray(v) for k, v in inputs.items()}
    w = {}
    w["mod"] = np.concatenate([by_rows(a["w_mod"][l], 2, 512) for l in range(2)])
    w["in_ab"] = by_feature(a["w_in_ab"][0])
    w["out_ab"] = by_feature(a["w_out_ab"][0])
    w["up"] = np.concatenate([by_feature(a["w_up"][l]) for l in range(2)])
    w["down"] = np.concatenate([by_feature(a["w_down"][l][h * HALF * P:(h + 1) * HALF * P])
                                for l in range(2) for h in range(2)])
    qkv = a["w_qkv"][0]
    w["qk"] = np.concatenate([by_feature(qkv[:, :1024][:, Q_ORDER]), by_feature(qkv[:, 1024:1280])])
    w["v"] = by_rows(qkv[:, 1280:1536], 4, 256)
    w["o"] = by_feature(a["w_o"][0][Q_ORDER])
    sizes = (1024, 2048, 16, 1536, 512, 768, 24, 3072)
    cuts = [sum(sizes[:i]) for i in range(len(sizes) + 1)]
    z, xbc, dt, sb, nq, nkv, ng, mg = (a["w_in_2"][0][:, cuts[i]:cuts[i + 1]] for i in range(8))
    w["z"] = by_rows(z, 2, 512)
    w["xbc"] = by_feature(xbc)
    w["dtg"] = by_rows(np.concatenate([dt, ng], axis=1), 8, 40)
    w["sbqk"] = by_feature(sb[:, :1024])
    w["sbv"] = by_rows(sb[:, 1024:], 2, 512)
    w["nq"] = by_feature(nq[:, NQ_ORDER])
    w["nk"] = by_feature(np.concatenate([nkv[:, 0:384], nkv[:, 512:640]], axis=1))
    w["nv"] = by_rows(np.concatenate([nkv[:, 384:512], nkv[:, 640:768]], axis=1), 4, 256)
    w["gate"] = by_feature(mg)
    w["br_ssm"] = by_feature(a["w_br_ssm_2"][0])
    w["br_sb"] = by_feature(a["w_br_sb_2"][0])
    w["br_nsa"] = by_feature(a["w_br_nsa_2"][0][NQ_ORDER])
    w["out2"] = by_feature(a["w_out_2"][0])
    w["up2"] = by_feature(a["ffn_w_up_2"][0])
    w["down2"] = np.concatenate([by_feature(a["ffn_w_down_2"][0][h * HALF * P:(h + 1) * HALF * P])
                                 for h in range(2)])

    def same(v):
        return np.broadcast_to(v.reshape(1, -1), (P, v.size))

    cond = np.stack([column(a["c"]), column(a["c_ctx"])], axis=2).reshape(P, 2 * KD)
    p = {
        "cond": cond, "b_mod": column(a["b_mod"]), "norm_mix": column(a["norm_mix"]),
        "norm_ffn": column(a["norm_ffn"]), "conv_a": column(a["conv_a"]), "conv_b": column(a["conv_b"]),
        "conv_b_bias": column(a["conv_b_bias"]), "ln_g": column(a["ln_b_gain"]),
        "ln_b": column(a["ln_b_bias"]), "conv_ffn": column(a["w_conv_ffn"]),
        "final_norm": column(a["final_norm"]), "pre_mix": column(a["pre_mix_norm_2"]),
        "ssm_conv_w": column(a["ssm_conv_w_2"]), "ssm_conv_b": column(a["ssm_conv_b_2"]),
        "ssm_norm": column(a["ssm_norm_2"]), "post_mix": column(a["post_mix_norm_2"]),
        "pre_ffn": column(a["pre_ffn_norm_2"]), "conv_ffn2": column(a["ffn_conv_w_2"]),
        "conv_ffn2_b": column(a["ffn_conv_b_2"]), "post_ffn": column(a["post_ffn_norm_2"]),
        "dt_bias": same(a["ssm_dt_bias_2"]), "a_log": same(a["ssm_a_log_2"]), "ssm_d": same(a["ssm_d_2"]),
        "sinks": same(a["sinks"]), "eps": np.full((P, 1), EPS, np.float32),
    }
    for n, width in PARAM_COLS:
        assert p[n].shape == (P, width), (n, p[n].shape, width)
    arrays = {"params": np.concatenate([p[n] for n, _ in PARAM_COLS], axis=1), "consts": constants()}
    arrays["x"] = np.concatenate([a["x"][0], a["ctx"][0]], axis=0).T.reshape(KD, P, TALL)
    for i, s in enumerate("kv"):
        w1 = a[f"cmp_w1_{s}_2"][0].reshape(CMP_LEN, HD, HD).transpose(1, 0, 2)
        b1 = np.zeros((P, CMP_LEN, P), np.float32)
        b2 = np.zeros((P, P), np.float32)
        for g in range(NSA_G):
            b1[g * HD:(g + 1) * HD, :, g * HD:(g + 1) * HD] = w1
            b2[g * HD:(g + 1) * HD, g * HD:(g + 1) * HD] = a[f"cmp_w2_{s}_2"][0]
        arrays[f"cmp_w1_{i}"] = b1.reshape(P, -1)
        arrays[f"cmp_w2_{i}"] = b2
        arrays[f"cmp_pos_{i}"] = np.concatenate([a[f"cmp_pos_{s}_2"][0].T] * NSA_G, axis=0)
    for n, v in w.items():
        count, kt, cols = WEIGHTS[n]
        assert v.shape == (count, P, kt * cols), (n, v.shape)
        arrays[n] = v
    arrays = {n: np.ascontiguousarray(v) for n, v in arrays.items()}

    nc = bacc.Bacc("TRN2", target_bir_lowering=False, num_devices=1)
    dram = {n: nc.dram_tensor(f"in_{n}", list(v.shape), F32, kind="ExternalInput").ap()
            for n, v in arrays.items()}
    dram["x_spill"] = nc.dram_tensor("x_spill", [KD, P, TX], F32, kind="Internal").ap()
    out = nc.dram_tensor("out_features", [KD, P, TX], F32, kind="ExternalOutput").ap()
    build(nc, dram, out)
    r = run_bass_kernel_spmd(nc, [{f"in_{n}": v for n, v in arrays.items()}], core_ids=[0])
    y = np.asarray(r.results[0]["out_features"])
    return np.ascontiguousarray(y.reshape(D, TX).T)[None]
```

```python
import numpy as np
import concourse.bass as bass
from concourse import mybir
from concourse.alu_op_type import AluOpType as ALU

ACT = mybir.ActivationFunctionType
F32 = mybir.dt.float32
F32R = mybir.dt.float32r
AX = mybir.AxisListType

P = 128
D = 1024
KD = D // P
TX, TC = 512, 256
TALL = TX + TC
SEG_BOTH = ((0, TX), (TX, TC))
SEG_X = ((0, TX),)
EPS = 1e-6
NEG = -1e30
FF = 2816
FFT = FF // P
PARTS = ((0, 8), (8, 8), (16, 6))
G_TILES = 9
SLOT = 8 * P

AW = 512
HD = 64
NH, NKV = 16, 4
BLK = 128
NBLK = TX // BLK
GRID_W = 64

SSM_H, SSM_G, SSM_N, SSM_P = 16, 4, 128, 64
SB_H = 4
NSA_H, NSA_G = 8, 2
CMP_STRIDE, CMP_LEN = 16, 32
NCMP = TX // CMP_STRIDE - 1
SLOPES = [2.0 ** (-8.0 * (h + 1) / NSA_H) for h in range(NSA_H)]

PARAM_COLS = [
    ("cond", 2 * KD), ("b_mod", 2 * 48), ("norm_mix", 2 * KD), ("norm_ffn", 2 * KD),
    ("conv_a", 3 * 4), ("conv_b", 31 * 4), ("conv_b_bias", 4), ("ln_g", 4), ("ln_b", 4),
    ("conv_ffn", 2 * 3 * 44), ("final_norm", KD), ("pre_mix", KD), ("ssm_conv_w", 4 * 16),
    ("ssm_conv_b", 16), ("ssm_norm", KD), ("post_mix", KD), ("pre_ffn", KD),
    ("conv_ffn2", 3 * 44), ("conv_ffn2_b", 44), ("post_ffn", KD),
    ("dt_bias", 16), ("a_log", 16), ("ssm_d", 16), ("sinks", 16), ("eps", 1),
]
CONST_COLS = [
    ("ident", 128), ("upto", 128), ("later", 128), ("neg_from", 128),
    ("neg_one", 128), ("before", 128), ("pick", 2),
    ("rope_rot", 128), ("cos", 512), ("sin", 512), ("window", 384),
    ("dist", 512), ("cmp_dist", 4 * NCMP), ("cmp_valid", 4 * NCMP),
]


def columns(table):
    at, out = 0, {}
    for name, width in table:
        out[name] = (at, width)
        at += width
    return out, at


PCOL, NPARAM = columns(PARAM_COLS)
CCOL, NCONST = columns(CONST_COLS)

WEIGHTS = {
    "mod": (2 * 48, 2, 512), "in_ab": (20, 8, 128), "out_ab": (8, 8, 128), "up": (88, 8, 128),
    "down": (32, 8, 128), "down_end": (16, 6, 128), "qk": (10, 8, 128), "v": (2, 4, 256), "o": (8, 8, 128),
    "z": (8, 2, 512), "xbc": (16, 8, 128), "dtg": (1, 8, 40), "sbqk": (8, 8, 128),
    "sbv": (4, 2, 512), "nq": (4, 8, 128), "nk": (4, 8, 128), "nv": (2, 4, 256),
    "gate": (24, 8, 128), "br_ssm": (8, 8, 128), "br_sb": (8, 4, 128), "br_nsa": (8, 4, 128),
    "out2": (8, 8, 128), "up2": (44, 8, 128), "down2": (16, 8, 128),
    "down2_end": (8, 6, 128),
}


class Engine:

    def __init__(self, nc, eng, name):
        self.eng = eng
        self.sem = nc.alloc_semaphore(f"done_{name}")
        self.count = 0
        self.waited = {}

    def after(self, *tokens):
        for tok in tokens:
            if tok is None:
                continue
            sem, value = tok
            if self.waited.get(id(sem), 0) < value:
                self.eng.wait_ge(sem, value)
                self.waited[id(sem)] = value

    def do(self, method, *args, after=(), **kw):
        self.after(*after)
        ins = method(*args, **kw)
        ins.then_inc(self.sem, 1)
        self.count += 1
        return (self.sem, self.count)


class Turn:

    def __init__(self, aps, numbers):
        self.aps = aps
        self.only(*numbers)

    def only(self, *numbers):
        self.numbers = numbers
        self.at = 0

    def next(self):
        i = self.numbers[self.at % len(self.numbers)]
        self.at += 1
        return i, self.aps[i]


def build(nc, dram, out, plan):
    recording = not plan
    pe = Engine(nc, nc.tensor, "pe")
    act = Engine(nc, nc.scalar, "act")
    dve = Engine(nc, nc.vector, "dve")
    pool = Engine(nc, nc.gpsimd, "pool")
    V, S, T, G = nc.vector, nc.scalar, nc.tensor, nc.gpsimd

    def sbuf(name, cols, dt=F32):
        return nc.alloc_sbuf_tensor(name, [P, cols], dt)[:, :]

    params = sbuf("params", NPARAM)
    resident = CCOL["rope_rot"][0]
    consts = sbuf("consts", resident)
    mods = [sbuf(f"mod{i}", 96).rearrange("p (c w) -> p c w", w=2) for i in range(2)]
    gain = sbuf("gain", 2 * KD).rearrange("p (k w) -> p k w", w=2)
    ssm_small = sbuf("ssm_small", 360)
    mean_ones = sbuf("mean_ones", P)
    rstd = sbuf("rstd", TALL)
    sq_sum = sbuf("sq_sum", TALL)
    NRAW, NHALF = 3, 3
    raw = [sbuf(f"w_raw{i}", SLOT) for i in range(NRAW)]
    w_hi = [sbuf(f"w_hi{i}", SLOT, F32R) for i in range(NHALF)]
    w_lo = [sbuf(f"w_lo{i}", SLOT, F32R) for i in range(NHALF)]
    mod_row = sbuf("mod_row", 512)
    scratch_bufs = [sbuf(f"scratch{i}", TALL) for i in range(5)]
    scratch = Turn(scratch_bufs, range(5))
    side = Turn(scratch_bufs, (3, 4))
    psum = nc.alloc_psum_tensor("psum", [P, 8 * 512], F32)[:, :]
    scratch_read = [()] * 5
    bank_read = [()] * 8
    bank_at = [0]

    in_turn = [0, 8]

    def next_banks(n=1):
        first, end = in_turn
        i = (bank_at[0] + n - 1) // n * n
        if i < first or i + n > end:
            i = (first + n - 1) // n * n
        bank_at[0] = i + n
        return i, bank_cols(i, n)

    def bank_cols(i, n=1):
        return psum[:, i * 512:(i + n) * 512]


    free_at = [(nc.sbuf_base + 63) // 64 * 64]
    top = nc.sbuf_usable_end

    def place(name, cols, dt=F32, at=None):
        where = free_at[0] if at is None else at
        assert where + 4 * cols <= top, (name, where + 4 * cols - top)
        if at is None:
            free_at[0] = (where + 4 * cols + 31) // 32 * 32
        return nc.alloc_sbuf_tensor_at(name, [P, cols], dt, offset=where)[:, :]

    def tiles(ap, width):
        return ap.rearrange("p (k t) -> p k t", t=width)

    cond_at = free_at[0]
    cond_w = place("cond_w", KD * P, F32R)
    x_at = free_at[0]
    xall = tiles(place("xall", KD * TALL), TALL)
    h_at = free_at[0]
    h_hi = tiles(place("h_hi", KD * TALL, F32R), TALL)
    h_lo = tiles(place("h_lo", KD * TALL, F32R), TALL)
    arena = free_at[0]

    def param(name, i=0, n=1):
        at, _ = PCOL[name]
        return params[:, at + i:at + i + n]

    def const(name):
        at, n = CCOL[name]
        return consts[:, at:at + n]

    def f32(ap):
        return ap.bitcast(F32)

    loaded = {}

    def load(what, dst, src, after=()):
        if what not in loaded:
            loaded[what] = [nc.alloc_semaphore(f"loaded_{what}"), 0]
        sem, n = loaded[what]
        loaded[what][1] = n + 1
        act.after(*after)
        S.dma_start(dst, src).then_inc(sem, 16)
        return (sem, 16 * (n + 1))

    p_in = load("params", params, dram["params"])
    c_in = load("consts", consts, dram["consts"][:, 0:resident])
    ident = const("ident")
    ones_ready = dve.do(V.memset, mean_ones, 1.0 / D)
    for e in (pe, act, dve):
        e.after(p_in, c_in, ones_ready)
    x_in = load("x", xall, dram["x"].rearrange("k p t -> p k t"))

    raw_sem = [nc.alloc_semaphore(f"loaded_raw{i}") for i in range(NRAW)]
    raw_read = []
    split = []
    used = []

    def split_piece(i):
        name, _ = plan[i]
        _, kt, n = WEIGHTS[name]
        r, q = i % NRAW, i % NHALF
        arrived = (raw_sem[r], 16 * (i // NRAW + 1))
        reuse = (used[i - NHALF],) if i >= NHALF else ()
        a = act.do(S.copy, w_hi[q][:, 0:kt * n], raw[r][:, 0:kt * n], after=(arrived, *reuse))
        e, eng = (dve, V) if i < 16 and i % 2 else (pool, G)
        b = e.do(eng.tensor_tensor, w_lo[q][:, 0:kt * n], raw[r][:, 0:kt * n],
                 f32(w_hi[q][:, 0:kt * n]), ALU.subtract, after=(arrived, a, *reuse))
        split.append((a, b))
        raw_read.append((a, b))

    next_piece = [0]

    def weight(name, idx):
        i = next_piece[0]
        next_piece[0] += 1
        if recording:
            plan.append((name, idx))
        assert plan[i] == (name, idx), (plan[i], name, idx)
        while len(split) < min(i + NHALF, len(plan)):
            split_piece(len(split))
        pe.after(*split[i])
        _, kt, n = WEIGHTS[name]
        q = i % NHALF
        return (w_hi[q][:, 0:kt * n].rearrange("p (k n) -> p k n", n=n),
                w_lo[q][:, 0:kt * n].rearrange("p (k n) -> p k n", n=n))

    def done_with_piece(tok):
        used.append(tok)

    def three_pass(dst, kt, stationary, moving, first=True, last=True):
        for k in range(kt):
            s_hi, s_lo = stationary(k)
            m_hi, m_lo = moving(k)
            for n, (a, b) in enumerate(((s_hi, m_hi), (s_hi, m_lo), (s_lo, m_hi))):
                start, stop = first and k == 0 and n == 0, last and k == kt - 1 and n == 2
                if stop:
                    return pe.do(T.matmul, dst, a, b, start=start, stop=True)
                if k == kt - 1 and n == 2:
                    return pe.do(T.matmul, dst, a, b, start=start, stop=False)
                T.matmul(dst, a, b, start=start, stop=False)

    def acts_of(hi, lo, ready, n=KD):
        return [(hi[:, k, :], lo[:, k, :], ready[k]) for k in range(n)]

    def product(name, idx, acts, segs, dst):
        _, kt, _ = WEIGHTS[name]
        hi, lo = weight(name, idx)
        for t0, n in segs:
            to = dst[:, t0:t0 + n]
            for k in range(kt):
                a_hi, a_lo, made = acts[k]
                if len(a_hi.shape) == 3:
                    to = dst[:, 0:TX].rearrange("p (c t) -> p c t", t=BLK)
                else:
                    a_hi, a_lo = a_hi[:, t0:t0 + n], a_lo[:, t0:t0 + n]
                pe.after(*made)
                tok = three_pass(to, 1, lambda _: (hi[:, k, :], lo[:, k, :]), lambda _: (a_hi, a_lo),
                                 first=k == 0, last=k == kt - 1)
        done_with_piece(tok)
        return tok

    def product_tokens(name, first_idx, acts, blocks, n, dsts):
        _, kt, _ = WEIGHTS[name]
        pieces = KD // kt
        for g in range(pieces):
            hi, lo = weight(name, first_idx + g)
            for b, dst in zip(blocks, dsts):
                cols = slice(b * BLK, (b + 1) * BLK)
                for k in range(kt):
                    a_hi, a_lo, made = acts[g * kt + k]
                    pe.after(*made)
                    tok = three_pass(dst, 1, lambda _: (a_hi[:, cols], a_lo[:, cols]),
                                     lambda _: (hi[:, k, :], lo[:, k, :]), first=g == 0 and k == 0,
                                     last=g == pieces - 1 and k == kt - 1)
            done_with_piece(tok)
        return tok

    def split_acts(dst_hi, dst_lo, src, after):
        a = act.do(S.copy, dst_hi, src, after=after)
        b = dve.do(V.tensor_tensor, dst_lo, src, f32(dst_hi), ALU.subtract, after=(a, *after))
        return a, b

    rstd_readers, sum_readers, gain_readers, h_readers = [()], [()], [()], [()]
    x_ready = [x_in]
    pending_sq = []

    def add_square(k, src, width, ready):
        if k == 0:
            act.after(*sum_readers[0])
            a = act.do(S.activation, sq_sum[:, 0:width], src, ACT.Square, after=ready)
            pending_sq[:] = [(None, None, a)]
            return
        i, sq = scratch.next()
        act.after(*scratch_read[i])
        a = act.do(S.activation, sq[:, 0:width], src, ACT.Square, after=ready)
        sum_square(width)
        pending_sq.append((i, sq, a))

    def sum_square(width):
        i, sq, a = pending_sq.pop()
        if sq is None:
            sum_ready[0] = a
            return
        sum_ready[0] = dve.do(V.tensor_tensor, sq_sum[:, 0:width], sq_sum[:, 0:width], sq[:, 0:width],
                              ALU.add, after=(a, sum_ready[0]))
        scratch_read[i] = (sum_ready[0],)

    sum_ready = [None]

    def finish_norm(segs):
        width = segs[-1][0] + segs[-1][1]
        sum_square(width)
        bank, ps = next_banks(2)
        pe.after(*bank_read[bank], *bank_read[bank + 1], sum_ready[0])
        for t0, n in segs:
            tok = pe.do(T.matmul, ps[:, t0:t0 + n], mean_ones, sq_sum[:, t0:t0 + n], start=True, stop=True)
        sum_readers[0] = (tok,)
        act.after(*rstd_readers[0])
        a = act.do(S.activation, rstd[:, 0:width], ps[:, 0:width], ACT.Sqrt, bias=param("eps"),
                   after=(tok,))
        bank_read[bank] = bank_read[bank + 1] = (a,)
        return dve.do(V.reciprocal, rstd[:, 0:width], rstd[:, 0:width], after=(a,))

    def modulated_norm(norm, layer, part, segs):
        mod, made = mods[layer], mod_ready[layer]
        n0 = PCOL[norm][0] + layer * KD
        g = params[:, n0:n0 + KD].unsqueeze(2).broadcast_to([P, KD, 2])
        tg = dve.do(V.scalar_tensor_tensor, gain, mod[:, (part + 1) * 8:(part + 2) * 8, :], 1.0, g,
                    ALU.add, ALU.mult, after=(made[part + 1], *gain_readers[0]))
        r = finish_norm(segs)
        ready, rests = [], []

        def rest(k, i, t, a):
            for who, (t0, n) in enumerate(segs):
                cols = slice(t0, t0 + n)
                b = dve.do(V.scalar_tensor_tensor, h_lo[:, k, cols], t[:, cols],
                           mod[:, part * 8 + k, who:who + 1], f32(h_hi[:, k, cols]), ALU.add,
                           ALU.subtract, after=(a, *h_readers[0]))
            scratch_read[i] = (a, b)
            ready.append((a, b))

        for k in range(KD):
            i, t = scratch.next()
            dve.after(*scratch_read[i])
            for who, (t0, n) in enumerate(segs):
                cols = slice(t0, t0 + n)
                m = dve.do(V.scalar_tensor_tensor, t[:, cols], xall[:, k, cols],
                           gain[:, k, who:who + 1], rstd[:, cols], ALU.mult, ALU.mult,
                           after=(tg, r, x_ready[0]))
                a = act.do(S.activation, h_hi[:, k, cols], t[:, cols], ACT.Identity,
                           bias=mod[:, part * 8 + k, who:who + 1],
                           after=(m, made[part], *h_readers[0]))
            rests.append((k, i, t, a))
            if k:
                rest(*rests[k - 1])
        rest(*rests[-1])
        rstd_readers[0] = gain_readers[0] = (m,)
        return acts_of(h_hi, h_lo, ready)

    mod_ready = [{}, {}]
    cond = scratch.aps[0][:, 0:2 * KD]
    cw = cond_w.rearrange("p (k m) -> p k m", m=P)
    z = dve.do(V.memset, f32(cond_w), 0.0)
    s = act.do(S.activation, cond, param("cond", 0, 2 * KD), ACT.Silu)
    c3 = cond.rearrange("p (k w) -> p k w", w=2)
    a = act.do(S.copy, cw[:, :, 0:2], c3, after=(z, s))
    cond_ready = dve.do(V.tensor_tensor, cw[:, :, 2:4], c3, f32(cw[:, :, 0:2]), ALU.subtract, after=(a,))
    scratch_read[0] = (a, cond_ready)
    row_read = [()]

    MOD_BANK = 6

    def adaln(layer):
        pick = const("pick")
        ps = bank_cols(MOD_BANK)
        for chunk in range(12):
            for g in range(4):
                hi, lo = weight("mod", layer * 48 + chunk * 4 + g)
                pe.after(*bank_read[MOD_BANK], cond_ready)
                for k in range(2):
                    T.matmul(ps, cw[:, 2 * g + k, :], hi[:, k, :], start=g == 0 and k == 0, stop=False)
                    tok = pe.do(T.matmul, ps, cw[:, 2 * g + k, :], lo[:, k, :], start=False,
                                stop=g == 3 and k == 1)
                done_with_piece(tok)
                if g < 3:
                    yield
            c = act.do(S.copy, mod_row[0:4, :], ps[0:4, :], after=(tok, *row_read[0]))
            bank_read[MOD_BANK] = (c,)
            yield
            pe.after(*bank_read[MOD_BANK], c)
            for j in range(4):
                tok = pe.do(T.matmul, ps[:, 2 * j:2 * j + 2], mod_row[0:4, j * P:(j + 1) * P],
                            pick[0:4, :], start=True, stop=True)
            row_read[0] = (tok,)
            bias = param("b_mod", layer * 48 + chunk * 4, 4).unsqueeze(2).broadcast_to([P, 4, 2])
            m = dve.do(V.tensor_tensor, mods[layer][:, chunk * 4:chunk * 4 + 4, :],
                       ps[:, 0:8].rearrange("p (c w) -> p c w", w=2), bias, ALU.add, after=(tok,))
            bank_read[MOD_BANK] = (m,)
            mod_ready[layer][chunk // 2] = m

    def steps(work, n=1):
        for _ in range(n):
            next(work, None)

    def add_gated(name, idxs, acts, layer, part, segs, squares=False, work=None):
        width = segs[-1][0] + segs[-1][1]
        for m, idx in enumerate(idxs):
            bank, ps = next_banks(2)
            pe.after(*bank_read[bank], *bank_read[bank + 1])
            tok = product(name, idx, acts, segs, ps)
            for who, (t0, n) in enumerate(segs):
                cols = slice(t0, t0 + n)
                d = dve.do(V.scalar_tensor_tensor, xall[:, m, cols], ps[:, cols],
                           mods[layer][:, part * 8 + m, who:who + 1], xall[:, m, cols], ALU.mult,
                           ALU.add, after=(tok, mod_ready[layer][part], x_ready[0]))
            bank_read[bank] = bank_read[bank + 1] = (d,)
            if squares:
                add_square(m, xall[:, m, 0:width], width, (d,))
            if work:
                steps(work)
        x_ready[0] = d
        return tok, d

    def conv3(src, seg_cols, taps, shifts, dst, ready, bias=None):
        lo, hi = seg_cols[0][0], seg_cols[-1][0] + seg_cols[-1][1]
        center = shifts.index(0)
        kw = {"bias": bias} if bias is not None else {}
        last = act.do(S.activation, dst[:, lo:hi], src[:, lo:hi], ACT.Identity, scale=taps[center],
                      after=ready, **kw)
        for tap, shift in zip(taps, shifts):
            if shift == 0:
                continue
            for t0, n in seg_cols:
                to = slice(t0 + max(shift, 0), t0 + n + min(shift, 0))
                of = slice(t0 + max(-shift, 0), t0 + n + min(-shift, 0))
                d = dve.do(V.scalar_tensor_tensor, dst[:, to], src[:, of], tap, dst[:, to],
                           ALU.mult, ALU.add, after=(last, *ready))
            last = d
        return last

    def ffn(up, base, acts, segs, g_hi, g_lo, g_free, conv_w, conv_b, shifts, gate_first, func, down,
            work=None):
        width = segs[-1][0] + segs[-1][1]
        made_g = {}
        slot_read = [g_free] * G_TILES

        def up_tile(t):
            made = []
            for side in range(2):
                tile = side * FFT + t
                bank, ps = next_banks(2)
                pe.after(*bank_read[bank], *bank_read[bank + 1])
                tok = product(up, base * 44 + tile, acts, segs, ps)
                i, u = scratch.next()
                act.after(*scratch_read[i])
                dve.after(*scratch_read[i])
                taps = [param(conv_w, (base * 3 + j) * 44 + tile) for j in range(3)]
                b = param(conv_b, tile) if conv_b else None
                d = conv3(ps, segs, taps, shifts, u, (tok,), bias=b)
                bank_read[bank] = bank_read[bank + 1] = (d,)
                made.append((i, u, d))
                if work and (side or t % 2):
                    steps(work)
            gate, value = (made[0], made[1]) if gate_first else (made[1], made[0])
            s = act.do(S.activation, gate[1][:, 0:width], gate[1][:, 0:width], func, after=(gate[2],))
            m = dve.do(V.tensor_tensor, value[1][:, 0:width], value[1][:, 0:width],
                       gate[1][:, 0:width], ALU.mult, after=(s, value[2]))
            q = t % G_TILES
            made_g[t] = split_acts(g_hi[:, q, 0:width], g_lo[:, q, 0:width], value[1][:, 0:width],
                                   (m, *slot_read[q]))
            scratch_read[gate[0]] = (m,)
            scratch_read[value[0]] = made_g[t]
            return tok

        done = 0
        for part, (t0, count) in enumerate(PARTS):
            while done < min(t0 + count + 1, FFT):
                h_used = up_tile(done)
                done += 1
            g_acts = [(g_hi[:, t % G_TILES, :], g_lo[:, t % G_TILES, :], made_g[t])
                      for t in range(t0, t0 + count)]
            tok = down(part, g_acts)
            for t in range(t0, t0 + count):
                slot_read[t % G_TILES] = (tok,)
        return tok, h_used

    def ffn_layer(layer, segs, readers, work=None):
        width = segs[-1][0] + segs[-1][1]
        acts = modulated_norm("norm_ffn", layer, 3, segs)
        g_hi = tiles(place(f"g_hi{layer}", G_TILES * width, F32R, at=arena), width)
        g_lo = tiles(place(f"g_lo{layer}", G_TILES * width, F32R, at=arena + 4 * G_TILES * width), width)

        def down(part, g_acts):
            name, first = ("down", layer * 16 + part * 8) if part < 2 else ("down_end", layer * 8)
            return add_gated(name, range(first, first + KD), g_acts, layer, 5, segs,
                             squares=part == 2)[0]

        tok, h_used = ffn("up", layer, acts, segs, g_hi, g_lo, readers, "conv_ffn", None, [1, 0, -1],
                          False, ACT.Silu, down, work)
        h_readers[0] = (h_used,)
        return (tok, x_ready[0])

    in_turn[:] = [0, 6]
    mod_work = adaln(0)
    for k in range(KD):
        steps(mod_work, 2)
        add_square(k, xall[:, k, :], TALL, (x_in,))
    steps(mod_work)
    h = modulated_norm("norm_mix", 0, 0, SEG_BOTH)
    released = ()

    PAD = 15
    UW = TALL + 4 * PAD
    CW = UW - 2 * PAD
    ya_hi = tiles(place("ya_hi", 4 * TALL, F32R, at=arena), TALL)
    ya_lo = tiles(place("ya_lo", 4 * TALL, F32R, at=arena + 16 * TALL), TALL)
    upad = tiles(place("upad", 4 * UW, at=arena + 32 * TALL), UW)
    conv = tiles(place("conv", 4 * CW, at=arena + 32 * TALL + 16 * UW), CW)
    yb_hi = tiles(place("yb_hi", 4 * TALL, F32R, at=h_at), TALL)
    yb_lo = tiles(place("yb_lo", 4 * TALL, F32R, at=h_at + 16 * TALL), TALL)
    u_cols = ((0, TX, PAD), (TX, TC, 3 * PAD))
    zeroed = dve.do(V.memset, upad, 0.0, after=released)
    u_done = []
    conv_done = {}

    def conv_b_taps():
        for t in range(4):
            w = lambda j: param("conv_b", j * 4 + t)
            d = dve.do(V.tensor_scalar, conv[:, t, :], upad[:, t, 0:CW], w(0), param("conv_b_bias", t),
                       ALU.mult, ALU.add, after=(u_done[t], *released))
            for j in range(1, 31):
                d = dve.do(V.scalar_tensor_tensor, conv[:, t, :], upad[:, t, j:j + CW], w(j),
                           conv[:, t, :], ALU.mult, ALU.add, after=(d,))
                if j % 5 == 0:
                    yield
            conv_done[t] = d
            yield

    taps_left = conv_b_taps()

    def some_taps(n):
        for _ in range(n):
            next(taps_left, None)

    for t in range(4):
        bank_v, ps_v = next_banks(2)
        pe.after(*bank_read[bank_v], *bank_read[bank_v + 1])
        tok_v = product("in_ab", 12 + t, h, SEG_BOTH, ps_v)
        bank_g, ps_g = next_banks(2)
        pe.after(*bank_read[bank_g], *bank_read[bank_g + 1])
        tok_g = product("in_ab", 16 + t, h, SEG_BOTH, ps_g)
        i, sg = scratch.next()
        act.after(*scratch_read[i])
        a = act.do(S.activation, sg, ps_g[:, 0:TALL], ACT.Sigmoid, after=(tok_g,))
        for t0, n, shift in u_cols:
            d = dve.do(V.tensor_tensor, upad[:, t, t0 + shift:t0 + shift + n], ps_v[:, t0:t0 + n],
                       sg[:, t0:t0 + n], ALU.mult, after=(tok_v, a, zeroed))
        scratch_read[i] = (d,)
        bank_read[bank_v] = bank_read[bank_v + 1] = (d,)
        bank_read[bank_g] = bank_read[bank_g + 1] = (a,)
        u_done.append(d)
        steps(mod_work)
        some_taps(3)

    mixed = []
    for t in range(4):
        bank_c, ps_c = next_banks(2)
        pe.after(*bank_read[bank_c], *bank_read[bank_c + 1])
        tok_c = product("in_ab", 4 + t, h, SEG_BOTH, ps_c)
        i, gc = scratch.next()
        act.after(*scratch_read[i])
        a = act.do(S.copy, gc, ps_c[:, 0:TALL], after=(tok_c,))
        bank_read[bank_c] = bank_read[bank_c + 1] = (a,)
        steps(mod_work)
        some_taps(2)
        bank_u, ps_u = next_banks(2)
        pe.after(*bank_read[bank_u], *bank_read[bank_u + 1])
        tok_u = product("in_ab", 8 + t, h, SEG_BOTH, ps_u)
        d = dve.do(V.tensor_tensor, gc, gc, ps_u[:, 0:TALL], ALU.mult, after=(tok_u, a))
        bank_read[bank_u] = bank_read[bank_u + 1] = (d,)
        steps(mod_work)
        some_taps(1)
        j, ca = scratch.next()
        act.after(*scratch_read[j])
        dve.after(*scratch_read[j])
        c = conv3(gc, SEG_BOTH, [param("conv_a", n * 4 + t) for n in range(3)], [1, 0, -1], ca, (d,))
        scratch_read[i] = (c,)
        bank_b, ps_b = next_banks(2)
        pe.after(*bank_read[bank_b], *bank_read[bank_b + 1])
        tok_b = product("in_ab", t, h, SEG_BOTH, ps_b)
        d = dve.do(V.tensor_tensor, ca, ca, ps_b[:, 0:TALL], ALU.mult, after=(tok_b, c))
        bank_read[bank_b] = bank_read[bank_b + 1] = (d,)
        ya = split_acts(ya_hi[:, t, :], ya_lo[:, t, :], ca, (d,))
        scratch_read[j] = ya
        mixed.append((ya_hi[:, t, :], ya_lo[:, t, :], ya))
        steps(mod_work)
        some_taps(1)
    h_readers[0] = (tok_b,)
    for _ in taps_left:
        pass
    steps(mod_work, 8)

    conv_cols = ((0, TX, 0), (TX, TC, 2 * PAD))

    def mean512(src, ready):
        bank, ps = next_banks(2)
        pe.after(*bank_read[bank], *bank_read[bank + 1])
        for t in range(4):
            pe.after(*ready(t))
            for t0, n, shift in conv_cols:
                tok = pe.do(T.matmul, ps[:, t0:t0 + n], mean_ones, src(t)[:, t0 + shift:t0 + shift + n],
                            start=t == 0, stop=t == 3)
        return bank, ps, tok

    bank, ps, tok = mean512(lambda t: conv[:, t, :], lambda t: (conv_done[t],))
    steps(mod_work, 4)
    centered = []
    for t in range(4):
        for t0, n, shift in conv_cols:
            c = conv[:, t, t0 + shift:t0 + shift + n]
            d = dve.do(V.scalar_tensor_tensor, c, ps[:, t0:t0 + n], -2.0, c, ALU.mult, ALU.add,
                       after=(tok, conv_done[t]))
        centered.append(d)
    bank_read[bank] = bank_read[bank + 1] = (d,)
    squares = []
    steps(mod_work, 2)
    for t in range(4):
        squares.append(act.do(S.activation, upad[:, t, 0:CW], conv[:, t, :], ACT.Square,
                              after=(centered[t], conv_done[t])))
    bank, ps, tok = mean512(lambda t: upad[:, t, :], lambda t: (squares[t],))
    a = act.do(S.activation, rstd, ps[:, 0:TALL], ACT.Sqrt, scale=2.0, bias=param("eps"),
               after=(tok, *rstd_readers[0]))
    bank_read[bank] = bank_read[bank + 1] = (a,)
    r = dve.do(V.reciprocal, rstd, rstd, after=(a,))
    for _ in mod_work:
        pass
    yb = []
    for t in range(4):
        i, s = scratch.next()
        dve.after(*scratch_read[i])
        for t0, n, shift in conv_cols:
            d = dve.do(V.tensor_tensor, s[:, t0:t0 + n], conv[:, t, t0 + shift:t0 + shift + n],
                       rstd[:, t0:t0 + n], ALU.mult, after=(r, centered[t]))
        a = act.do(S.activation, s, s, ACT.Silu, scale=param("ln_g", t), bias=param("ln_b", t), after=(d,))
        yb = split_acts(yb_hi[:, t, :], yb_lo[:, t, :], s, (a, *h_readers[0]))
        scratch_read[i] = yb
        mixed.append((yb_hi[:, t, :], yb_lo[:, t, :], yb))
    rstd_readers[0] = (d,)

    tok, _ = add_gated("out_ab", range(KD), mixed, 0, 2, SEG_BOTH, squares=True)
    h_readers[0] = (tok,)
    mod_work = adaln(1)
    released = ffn_layer(0, SEG_BOTH, (tok, d), mod_work)
    assert 1 in mod_ready[1]
    free_at[0] = arena
    qT = tiles(place("qT", 8 * TX), TX)
    kT = tiles(place("kT", 2 * TALL), TALL)
    v_tok = tiles(place("v_tok", 6 * 256), 256)
    rope_at = free_at[0]
    rope_rot = place("rope_rot", P, at=rope_at)
    cos_t, sin_t = (place(n, TX, at=rope_at + 4 * (P + i * TX)) for i, n in enumerate(("cos", "sin")))
    rows = [place(f"scores{i}", 4 * 640) for i in range(3)]
    window = place("window", 384)
    smalls = [place(f"small{i}", 32) for i in range(3)]

    def load_const(what, dst, name, after):
        at, n = CCOL[name]
        return load(what, dst, dram["consts"][:, at:at + n], after=after)

    for dst, name in ((rope_rot, "rope_rot"), (cos_t, "cos"), (sin_t, "sin"), (window, "window")):
        c_in = load_const("attention_tables", dst, name, released)
    h = modulated_norm("norm_mix", 1, 0, SEG_BOTH)
    for e in (pe, act, dve):
        e.after(c_in, *released)

    got = [next_banks() for _ in range(6)]
    for bank, _ in got:
        pe.after(*bank_read[bank])
    tok = product_tokens("v", 0, h, range(6), 256, [ps[:, 0:256] for _, ps in got])
    for b, (bank, ps) in enumerate(got):
        v_ready = act.do(S.copy, v_tok[:, b, :], ps[:, 0:256], after=(tok,))
        bank_read[bank] = (v_ready,)

    def rotary(dst, name, idx, segs, scale):
        bank, ps = next_banks(2)
        pe.after(*bank_read[bank], *bank_read[bank + 1])
        tok = product(name, idx, h, segs, ps)
        i, q = scratch.next()
        act.after(*scratch_read[i])
        a = act.do(S.activation, q[:, 0:TX], ps[:, 0:TX], ACT.Copy, scale=scale, after=(tok,))
        if len(segs) > 1:
            a = act.do(S.copy, dst[:, TX:TALL], ps[:, TX:TALL], after=(tok,))
        bank_read[bank] = bank_read[bank + 1] = (a,)
        bank, ps = next_banks()
        pe.after(*bank_read[bank])
        r = pe.do(T.matmul, ps, rope_rot, q[:, 0:TX], start=True, stop=True, after=(a,))
        j, s = scratch.next()
        dve.after(*scratch_read[j])
        d1 = dve.do(V.tensor_tensor, s[:, 0:TX], ps, sin_t, ALU.mult, after=(r,))
        bank_read[bank] = (d1,)
        d2 = dve.do(V.tensor_tensor, q[:, 0:TX], q[:, 0:TX], cos_t, ALU.mult, after=(a, r))
        d3 = dve.do(V.tensor_tensor, dst[:, 0:TX], q[:, 0:TX], s[:, 0:TX], ALU.add, after=(d1, d2))
        scratch_read[i] = (d3,)
        scratch_read[j] = (d3,)
        return tok, d3, a

    for i in range(2):
        _, k_ready, kc_ready = rotary(kT[:, i, :], "qk", 8 + i, SEG_BOTH, 1.0)
    for i in range(8):
        h_used, q_ready, _ = rotary(qT[:, i, :], "qk", i, SEG_X, HD ** -0.5)
    pe.after(k_ready, kc_ready, q_ready, v_ready)

    O_BANK = 7
    at_hi = tiles(place("at_hi", KD * TX, F32R, at=h_at), TX)
    at_lo = tiles(place("at_lo", KD * TX, F32R, at=h_at + 4 * KD * TX), TX)

    class Unit:
        pass

    def exponents(u, sink=None):
        mx, neg, tot, _, snk = (u.small[:, 4 * i:4 * i + 4] for i in range(5))
        for two in (slice(0, 2), slice(2, 4)):
            d = dve.do(V.tensor_reduce, mx[:, two], u.s[:, two, :], AX.X, ALU.max, after=(*u.ready,))
            yield
        if sink is not None:
            d = dve.do(V.tensor_tensor, mx, mx, sink, ALU.max, after=(d,))
        n = dve.do(V.tensor_scalar, neg, mx, -1.0, None, ALU.mult, after=(d,))
        if sink is not None:
            k = dve.do(V.tensor_tensor, snk, sink, mx, ALU.subtract, after=(d,))
            u.sink_exp = act.do(S.activation, snk, snk, ACT.Exp, after=(k,))
        for h in range(4):
            e = act.do(S.activation, u.s[:, h, :], u.s[:, h, :], ACT.Exp, bias=neg[:, h:h + 1],
                       accum_out=tot[:, h:h + 1], after=(n, *u.ready))
            yield
        u.exps = e

    def divide(u, gates=None, valid=None, sink=None):
        _, _, tot, rec, snk = (u.small[:, 4 * i:4 * i + 4] for i in range(5))
        t = e = u.exps
        if sink is not None:
            t = dve.do(V.tensor_tensor, tot, tot, snk, ALU.add, after=(e, u.sink_exp))
        r = dve.do(V.reciprocal, rec, tot, after=(t,))
        if gates is not None:
            r = dve.do(V.tensor_tensor, rec, rec, gates, ALU.mult, after=(r,))
        for h in range(4):
            d = dve.do(V.tensor_scalar, u.s[:, h, :], u.s[:, h, :], rec[:, h:h + 1], None, ALU.mult,
                       after=(r, e))
            if h == 1:
                yield
        if valid is not None:
            d = dve.do(V.tensor_tensor, u.s, u.s, valid, ALU.mult, after=(d,))
        u.soft = d
        yield

    def turn(u, c0, n):
        bank, ps = next_banks()
        pe.after(*bank_read[bank])
        pe.after(u.soft)
        for h in range(4):
            t = pe.do(T.transpose, ps[0:n, h * P:(h + 1) * P], u.s[:, h, c0:c0 + n], ident)
        e = (act, dve)[len(u.turned) % 2]
        i, pt = scratch.next()
        e.after(*scratch_read[i])
        pt = pt[:, 0:512]
        c = e.do(S.copy if e is act else V.tensor_copy, pt[0:n, :], ps[0:n, :], after=(t,))
        bank_read[bank] = (c,)
        u.turned.append((i, pt, n, c, t))

    def apply(u, between):
        if u.first:
            pe.after(*bank_read[O_BANK])
        o = psum[0:HD, O_BANK * 512:(O_BANK + 1) * 512]
        turned = u.turned
        for j, (c0, n, v) in enumerate(u.keys):
            if j + 1 < len(u.keys):
                turn(u, *u.keys[j + 1][:2])
            i, pt, n, c, _ = turned[j]
            m = pe.do(T.matmul, o, v, pt[0:n, :], start=u.first and j == 0,
                      stop=u.last and j == len(u.keys) - 1, after=(c,))
            scratch_read[i] = (m,)
            steps(between)
        u.read = turned[-1][4]
        if u.last:
            dst_hi, dst_lo = u.dst
            src = o.rearrange("p (h q) -> p h q", q=P)
            a = act.do(S.copy, dst_hi, src, after=(m, *u.dst_free))
            b = dve.do(V.tensor_tensor, dst_lo, src, f32(dst_hi), ALU.subtract, after=(a, *u.dst_free))
            bank_read[O_BANK] = (a, b)
            return a, b
        return None

    def run_units(units, scores, exps, softmax, rows, rows_free=(), work=None, per_unit=1, every=1, pause=0):
        ahead = len(rows) - 1
        done = ()
        for n in range(len(units) + ahead):
            if n < len(units):
                u = units[n]
                u.rows, u.small = rows[n % len(rows)], smalls[n % len(rows)]
                u.free = (units[n - len(rows)].read,) if n >= len(rows) else rows_free
                u.turned = []
                making = scores(u)
                next(making)
            if n >= ahead:
                turn(units[n - ahead], *units[n - ahead].keys[0][:2])
            if n < len(units):
                for _ in making:
                    pass

            def softmax_steps():
                if 0 < n <= len(units):
                    yield from softmax(units[n - 1])
                if n < len(units):
                    yield from exps(units[n])

            rest = softmax_steps()
            if n >= ahead:
                if work and n >= pause:
                    steps(work, per_unit if (n - pause) % every == 0 else 0)
                done = apply(units[n - ahead], rest) or done
            for _ in rest:
                pass
        for _ in work or ():
            pass
        return done

    units = []
    for blk in range(NBLK):
        for g in range(NKV):
            u = Unit()
            u.blk, u.g = blk, g
            u.first = u.last = True
            near = [b for b in (blk - 1, blk, blk + 1) if 0 <= b < NBLK]
            u.near = near
            u.local = len(near) * BLK
            vs = [v_tok[:, b, g * HD:(g + 1) * HD] for b in near + [4, 5]]
            u.keys = [(i * BLK, BLK, v) for i, v in enumerate(vs)]
            half, base = g % 2, 4 * (g // 2)
            rows_ = slice(half * HD, half * HD + HD)
            u.dst = tuple(a[rows_, base:base + 4, blk * BLK:(blk + 1) * BLK] for a in (at_hi, at_lo))
            u.dst_free = (h_used,)
            units.append(u)

    def window_scores(u):
        half, base = u.g % 2, 4 * (u.g // 2)
        on = slice(half * HD, half * HD + HD)
        L = u.local + TC
        u.s = u.rows[:, 0:4 * L].rearrange("p (h l) -> p h l", l=L)
        cols = slice(u.near[0] * BLK, (u.near[-1] + 1) * BLK)
        shown = window[:, (u.near[0] - u.blk + 1) * BLK:(u.near[-1] - u.blk + 2) * BLK]
        q = lambda h: qT[on, base + h, u.blk * BLK:(u.blk + 1) * BLK]
        for pair in range(2):
            bank, ps = next_banks()
            pe.after(*bank_read[bank])
            for h in range(2):
                t = pe.do(T.matmul, ps[:, h * TC:(h + 1) * TC], q(2 * pair + h), kT[on, u.g // 2, TX:TALL],
                          start=True, stop=True)
            a = act.do(S.copy, u.s[:, 2 * pair:2 * pair + 2, u.local:L],
                       ps.rearrange("p (h l) -> p h l", l=TC), after=(t, *u.free))
            bank_read[bank] = (a,)
        for h in range(4):
            if h == 2:
                yield
            bank, ps = next_banks()
            pe.after(*bank_read[bank])
            t = pe.do(T.matmul, ps[:, 0:u.local], q(h), kT[on, u.g // 2, cols], start=True, stop=True)
            d = dve.do(V.tensor_tensor, u.s[:, h, 0:u.local], ps[:, 0:u.local], shown, ALU.add,
                       after=(t, *u.free))
            bank_read[bank] = (d,)
        u.ready = (a, d)

    def window_exps(u):
        return exponents(u, sink=param("sinks", 4 * u.g, 4))

    def window_softmax(u):
        return divide(u, sink=param("sinks", 4 * u.g, 4))

    at_done = run_units(units, window_scores, window_exps, window_softmax, rows, (q_ready,), mod_work, per_unit=3)
    in_turn[:] = [0, 8]
    tok, _ = add_gated("o", range(KD), acts_of(at_hi, at_lo, [at_done] * KD), 1, 2, SEG_X, squares=True)
    h_readers[0] = (tok,)
    released = ffn_layer(1, SEG_X, (tok, *at_done, units[-1].read))

    r = finish_norm(SEG_X)
    for k in range(KD):
        d = dve.do(V.scalar_tensor_tensor, xall[:, k, 0:TX], xall[:, k, 0:TX], param("final_norm", k),
                   rstd[:, 0:TX], ALU.mult, ALU.mult, after=(r, x_ready[0]))
        add_square(k, xall[:, k, 0:TX], TX, (d,))
    rstd_readers[0] = (d,)
    x_ready[0] = d

    stored = nc.alloc_semaphore("stored_x")
    act.after(x_ready[0])
    S.dma_start(dram["x_spill"].rearrange("k p t -> p k t"), xall[:, :, 0:TX]).then_inc(stored, 16)
    x_stored = (stored, 16)

    g_hi2 = tiles(place("h2_hi", KD * TX, F32R, at=h_at), TX)
    g_lo2 = tiles(place("h2_lo", KD * TX, F32R, at=h_at + 4 * KD * TX), TX)

    def plain_norm(src, name, ready, readers):
        r = finish_norm(SEG_X)
        made, rests = [], []

        def rest(k, i, t, a):
            b = dve.do(V.tensor_tensor, g_lo2[:, k, :], t[:, 0:TX], f32(g_hi2[:, k, :]), ALU.subtract,
                       after=(a, *readers))
            scratch_read[i] = (a, b)
            made.append((a, b))

        for k in range(KD):
            i, t = scratch.next()
            dve.after(*scratch_read[i])
            d = dve.do(V.scalar_tensor_tensor, t[:, 0:TX], src(k), param(name, k), rstd[:, 0:TX],
                       ALU.mult, ALU.mult, after=(r, ready))
            a = act.do(S.copy, g_hi2[:, k, :], t[:, 0:TX], after=(d, *readers))
            rests.append((k, i, t, a))
            if k:
                rest(*rests[k - 1])
        rest(*rests[-1])
        rstd_readers[0] = (d,)
        return acts_of(g_hi2, g_lo2, made)

    h2 = plain_norm(lambda k: xall[:, k, 0:TX], "pre_mix", x_ready[0], released)

    arena2 = h_at + 8 * KD * TX
    KB8 = 8192

    def at_a(i):
        return arena2 + i * KB8

    def at_x(i):
        return x_at + i * KB8

    sb_hi = tiles(place("sb_hi", SB_H * TX, F32R, at=at_a(0)), TX)
    sb_lo = tiles(place("sb_lo", SB_H * TX, F32R, at=at_a(1)), TX)
    x_tok = tiles(place("x_tok", NBLK * D, at=at_a(2)), D)
    b_tok = tiles(place("b_tok", NBLK * 512, at=at_a(4)), 512)
    bT = tiles(place("bT", 4 * TX, at=at_a(5)), TX)
    cT = tiles(place("cT", 4 * TX, at=at_a(8)), TX)
    sb_qT = tiles(place("sb_qT", SB_H * TX, at=at_a(6)), TX)
    sb_kT = tiles(place("sb_kT", SB_H * TX, at=at_a(7)), TX)
    sb_v = tiles(place("sb_v", NBLK * 512, at=at_x(0)), 512)
    sp = tiles(place("softplus_z", NBLK * TX, at=at_x(1)), TX)
    wgt = tiles(place("sb_w", NBLK * TX, at=at_x(2)), TX)
    scratch.only(0, 1, 2)

    for m in range(8):
        bank, ps = next_banks()
        pe.after(*bank_read[bank])
        tok = product("sbqk", m, h2, SEG_X, ps)
        dst = (sb_qT if m < 4 else sb_kT)[:, m % 4, :]
        a = act.do(S.activation, dst, ps, ACT.Copy, scale=128 ** -0.5 if m < 4 else 1.0,
                   after=(tok, *released))
        bank_read[bank] = (a,)
    qk_ready = a
    got = [next_banks() for _ in range(4)]
    for bank, _ in got:
        pe.after(*bank_read[bank])
    tok = product_tokens("sbv", 0, h2, range(4), 512, [ps for _, ps in got])
    for c, (bank, ps) in enumerate(got):
        a = act.do(S.copy, sb_v[:, c, :], ps, after=(tok, x_stored, *released))
        bank_read[bank] = (a,)
    pe.after(qk_ready, a)
    dve.after(*released, x_stored)
    act.after(*released, x_stored)
    xbc_done = {}

    def turn_tile(src, ready, dst, slot):
        bank, ps = next_banks()
        pe.after(*bank_read[bank])
        for c in range(4):
            t = pe.do(T.transpose, ps[:, c * P:(c + 1) * P], src[:, c * P:(c + 1) * P], ident,
                      after=(ready,))
        a = act.do(S.copy, dst, ps.rearrange("p (c f) -> p c f", f=P), after=(t, *released))
        bank_read[bank] = (a,)
        if slot is not None:
            scratch_read[slot] = (t,)
        return a

    def make_xbc():
        pending = None
        for m in range(16):
            bank, ps = next_banks()
            pe.after(*bank_read[bank])
            tok = product("xbc", m, h2, SEG_X, ps)
            i, u = side.next()
            act.after(*scratch_read[i])
            dve.after(*scratch_read[i])
            taps = [param("ssm_conv_w", j * 16 + m) for j in range(4)]
            d = conv3(ps, SEG_X, taps, [3, 2, 1, 0], u, (tok,), bias=param("ssm_conv_b", m))
            bank_read[bank] = (d,)
            if m < 8:
                a = act.do(S.activation, u[:, 0:TX], u[:, 0:TX], ACT.Silu, after=(d,))
            elif m < 12:
                a = act.do(S.activation, bT[:, m - 8, :], u[:, 0:TX], ACT.Silu, after=(d, *released))
                scratch_read[i] = (a,)
            else:
                a = act.do(S.activation, cT[:, m - 12, :], u[:, 0:TX], ACT.Silu, after=(d, *released))
                scratch_read[i] = (a,)
            if pending:
                xbc_done["tok"] = turn_tile(*pending)
            if m < 8:
                pending = (u, a, x_tok[:, :, m * P:(m + 1) * P], i)
            elif m < 12:
                pending = (bT[:, m - 8, :], a, b_tok[:, :, (m - 8) * P:(m - 7) * P], None)
            else:
                pending = None
            yield
        xbc_done["c"] = a

    xbc_work = make_xbc()
    w_read = ()
    in_turn[:] = [4, 8]
    for h in range(SB_H):
        held = []
        for kb in range(NBLK):
            n = TX - kb * BLK
            bank, ps = kb, bank_cols(kb)
            pe.after(*bank_read[bank])
            t = pe.do(T.matmul, ps[:, 0:n], sb_kT[:, h, kb * BLK:(kb + 1) * BLK],
                      sb_qT[:, h, kb * BLK:TX], start=True, stop=True)
            s = sp[:, kb, 0:n]
            d = dve.do(V.tensor_scalar, s, ps[:, 0:n], -1.0, None, ALU.mult, after=(t, *w_read))
            d = dve.do(V.tensor_tensor, s, ps[:, 0:n], s, ALU.min, after=(d,))
            a = act.do(S.activation, s, s, ACT.Exp, after=(d,))
            held.append((ps, s, a, n))
        logs = [act.do(S.activation, s, s, ACT.Ln, bias=1.0, after=(a,)) for _, s, a, _ in held]
        summed = []
        for (ps, s, _, n), a in zip(held, logs):
            d = dve.do(V.scalar_tensor_tensor, s, ps[:, 0:n], 0.0, s, ALU.max, ALU.add, after=(a,))
            summed.append(dve.do(V.tensor_tensor, s[:, 0:BLK], s[:, 0:BLK], const("before"), ALU.mult,
                                 after=(d,)))
        steps(xbc_work, 2)
        weighted = [None] * NBLK
        for kb in range(NBLK - 1, -1, -1):
            ps = held[kb][0]
            for kb2 in range(kb, NBLK):
                q0 = (kb2 - kb) * BLK
                t = pe.do(T.matmul, ps[:, q0:TX - kb * BLK], const("neg_from" if kb2 == kb else "neg_one"),
                          sp[:, kb2, 0:TX - kb2 * BLK], start=False, stop=kb2 == NBLK - 1,
                          skip_group_check=True, after=(*summed,))
            n = TX - kb * BLK
            a = act.do(S.activation, wgt[:, kb, 0:n], ps[:, 0:n], ACT.Exp, after=(t, *w_read))
            bank_read[kb] = (a,)
            d = dve.do(V.tensor_tensor, wgt[:, kb, 0:BLK], wgt[:, kb, 0:BLK], const("before"), ALU.mult,
                       after=(a,))
            weighted[kb] = (a, d)
        steps(xbc_work, 2)
        sp_read = t
        bank, ps = next_banks()
        pe.after(*bank_read[bank])
        for kb in range(NBLK):
            t = pe.do(T.matmul, ps[:, kb * BLK:TX], sb_v[:, kb, h * P:(h + 1) * P],
                      wgt[:, kb, 0:TX - kb * BLK], start=kb == 0, stop=kb == NBLK - 1,
                      after=weighted[kb])
        w_read = (sp_read, t)
        sb_done = split_acts(sb_hi[:, h, :], sb_lo[:, h, :], ps, (t, *released))
        bank_read[bank] = sb_done
    in_turn[:] = [0, 8]
    for _ in xbc_work:
        pass
    sb_over = (*sb_done, t)

    z_tok = tiles(place("z_tok", NBLK * D, at=at_x(0)), D)
    x_dt = place("x_dt", D, at=at_x(2))
    state = tiles(place("state", SSM_G * 256, at=at_x(2) + 4096), 256)
    ch = place("carried", D, at=cond_at)
    ssm_hi = place("ssm_hi", NBLK * D, F32R, at=at_a(2)).rearrange("p (c k t) -> p c k t", k=KD, t=BLK)
    ssm_lo = place("ssm_lo", NBLK * D, F32R, at=at_x(0)).rearrange("p (c k t) -> p c k t", k=KD, t=BLK)
    dt_t = ssm_small[:, 0:64].rearrange("p (c h) -> p c h", h=16)
    dta = ssm_small[:, 64:128].rearrange("p (c h) -> p c h", h=16)
    tmp64 = ssm_small[:, 128:192].rearrange("p (c h) -> p c h", h=16)
    a_neg = ssm_small[:, 192:208]
    e_acum = ssm_small[:, 208:224]
    to_end = ssm_small[:, 224:240]
    e_last = ssm_small[:, 240:256]
    gates = ssm_small[:, 256:352].rearrange("p (c h) -> p c h", h=24)
    gsum = ssm_small[:, 352:356]
    grec = ssm_small[:, 356:360]

    got = [next_banks() for _ in range(4)]
    for bank, _ in got:
        pe.after(*bank_read[bank])
    tok = product_tokens("dtg", 0, h2, range(4), 40, [ps[:, 0:40] for _, ps in got])
    for c, (bank, ps) in enumerate(got):
        d = dve.do(V.tensor_tensor, dt_t[:, c, :], ps[:, 0:16], param("dt_bias", 0, 16), ALU.add,
                   after=(tok,))
        gates_ready = act.do(S.activation, gates[:, c, :], ps[:, 16:40], ACT.Sigmoid, after=(tok, d))
        bank_read[bank] = (d, gates_ready)
    d1 = dve.do(V.tensor_scalar, tmp64, dt_t, -1.0, None, ALU.mult, after=(d,))
    d1 = dve.do(V.tensor_tensor, tmp64, tmp64, dt_t, ALU.min, after=(d1,))
    a = act.do(S.activation, tmp64, tmp64, ACT.Exp, after=(d1,))
    a = act.do(S.activation, tmp64, tmp64, ACT.Ln, bias=1.0, after=(a,))
    d = dve.do(V.scalar_tensor_tensor, dt_t, dt_t, 0.0, tmp64, ALU.max, ALU.add, after=(a,))
    a = act.do(S.activation, a_neg, param("a_log", 0, 16), ACT.Exp)
    d1 = dve.do(V.tensor_scalar, a_neg, a_neg, -1.0, None, ALU.mult, after=(a,))
    dt_ready = dve.do(V.tensor_tensor, dta, dt_t, a_neg.unsqueeze(1).broadcast_to([P, 4, 16]), ALU.mult,
                      after=(d, d1))

    z_ready = [None, None]

    def make_z():
        for half in range(2):
            got = [next_banks() for _ in range(4)]
            for bank, _ in got:
                pe.after(*bank_read[bank])
            tok = product_tokens("z", half * 4, h2, range(4), 512, [ps for _, ps in got])
            for c, (bank, ps) in enumerate(got):
                z_ready[half] = act.do(S.activation, z_tok[:, c, half * 512:(half + 1) * 512], ps,
                                       ACT.Silu, after=(tok, *sb_over))
                bank_read[bank] = (z_ready[half],)
            yield

    for e in (pe, dve):
        e.after(xbc_done["tok"], xbc_done["c"], dt_ready, *sb_over)

    nq = tiles(place("nq", 4 * TX, at=at_a(4)), TX)
    nk = tiles(place("nk", 2 * TX, at=at_a(6)), TX)
    nv = tiles(place("nv", NBLK * 256, at=at_a(6) + 4096), 256)
    w1 = [place(f"cmp_w1_half{i}", 8 * P, at=at_a(7) + 4096 * i).rearrange("p (l o) -> p l o", o=P)
          for i in range(2)]
    free_at[0] = at_a(9)
    kc = place("kc", 32)
    vc = place("vc", P)
    w2 = place("cmp_w2", P)
    pos = place("cmp_pos", CMP_LEN)
    hid = place("cmp_hidden", 32)
    cd_t = place("cmp_dist", 4 * NCMP).rearrange("p (b n) -> p b n", n=NCMP)
    cv_t = place("cmp_valid", 4 * NCMP).rearrange("p (b n) -> p b n", n=NCMP)
    smalls = [place(f"nsmall{i}", 32) for i in range(2)] + [mod_row[:, 128:160]]
    late_at = free_at[0]
    pos_blocks = tiles(place("cmp_blocks", CMP_LEN * NCMP), NCMP)
    load_const("sparse_tables", cd_t.rearrange("p b n -> p (b n)"), "cmp_dist", released)
    load_const("sparse_tables", cv_t.rearrange("p b n -> p (b n)"), "cmp_valid", released)
    sparse = {}

    def make_sparse():
        w1_read = [sb_over, sb_over]
        small_read = ()
        n_w1 = 0
        for which in range(2):
            w2_in = load("cmp_w2", w2, dram[f"cmp_w2_{which}"], after=small_read)
            pos_in = load("cmp_pos", pos, dram[f"cmp_pos_{which}"], after=small_read)
            bank, ps = next_banks()
            pe.after(*bank_read[bank])
            tok = product("nk", which, h2, SEG_X, ps)
            i, s = side.next()
            act.after(*scratch_read[i])
            a = act.do(S.copy, s[:, 0:TX], ps, after=(tok,))
            bank_read[bank] = (a,)
            for lh in range(2):
                src = s[:, lh * 16:lh * 16 + NCMP * 16].rearrange("p (n l) -> p l n", l=16)
                d = dve.do(V.tensor_tensor, pos_blocks[:, lh * 16:lh * 16 + 16, :], src,
                           pos[:, lh * 16:lh * 16 + 16].unsqueeze(2).broadcast_to([P, 16, NCMP]),
                           ALU.add, after=(a, pos_in, *small_read))
            scratch_read[i] = (d,)
            arrived = []
            for quarter in range(2):
                arrived.append(load(f"cmp_w1_{quarter}", w1[quarter].rearrange("p l o -> p (l o)"),
                                    dram[f"cmp_w1_{which}"][:, quarter * 1024:(quarter + 1) * 1024],
                                    after=w1_read[quarter]))
            yield
            bank, ps = next_banks()
            pe.after(*bank_read[bank], d, w2_in)
            for quarter in range(4):
                q = quarter % 2
                pe.after(arrived[quarter])
                for l in range(8):
                    t = pe.do(T.matmul, ps[:, quarter * 32:quarter * 32 + NCMP], w1[q][:, l, :],
                              pos_blocks[:, 8 * quarter + l, :], start=l == 0, stop=l == 7)
                w1_read[q] = (t,)
                if quarter < 2:
                    arrived.append(load(f"cmp_w1_{q}", w1[q].rearrange("p l o -> p (l o)"),
                                        dram[f"cmp_w1_{which}"][:, (quarter + 2) * 1024:(quarter + 3) * 1024],
                                        after=(t,)))
            d = dve.do(V.tensor_reduce, hid[:, 0:NCMP],
                       ps[:, 0:128].rearrange("p (q n) -> p n q", n=32)[:, 0:NCMP, :], AX.X, ALU.add,
                       after=(t, *small_read))
            bank_read[bank] = (d,)
            a = act.do(S.activation, hid[:, 0:NCMP], hid[:, 0:NCMP], ACT.Silu, after=(d,))
            yield
            bank, ps = next_banks()
            pe.after(*bank_read[bank])
            if which == 0:
                t = pe.do(T.matmul, ps[:, 0:NCMP], w2, hid[:, 0:NCMP], start=True, stop=True, after=(a,))
                a = act.do(S.copy, kc[:, 0:NCMP], ps[:, 0:NCMP], after=(t, *released))
            else:
                t = pe.do(T.matmul, ps[0:NCMP, 0:P], hid[:, 0:NCMP], w2, start=True, stop=True, after=(a,))
                a = act.do(S.copy, vc[0:NCMP, :], ps[0:NCMP, 0:P], after=(t, *released))
            bank_read[bank] = (a,)
            small_read = (t, a)
            yield
        for m in (2, 3):
            bank, ps = next_banks()
            pe.after(*bank_read[bank])
            tok = product("nk", m, h2, SEG_X, ps)
            a = act.do(S.copy, nk[:, m - 2, :], ps, after=(tok, *sb_over))
            bank_read[bank] = (a,)
            yield
        got = [next_banks() for _ in range(4)]
        for bank, _ in got:
            pe.after(*bank_read[bank])
        tok = product_tokens("nv", 0, h2, range(4), 256, [ps[:, 0:256] for _, ps in got])
        for c, (bank, ps) in enumerate(got):
            a = act.do(S.copy, nv[:, c, :], ps[:, 0:256], after=(tok, *sb_over))
            bank_read[bank] = (a,)
        sparse["ready"] = (a, *small_read)
        yield

    def make_queries():
        for m in range(4):
            bank, ps = next_banks()
            pe.after(*bank_read[bank])
            tok = product("nq", m, h2, SEG_X, ps)
            sparse["q"] = act.do(S.activation, nq[:, m, :], ps, ACT.Copy, scale=HD ** -0.5,
                                 after=(tok, b_tok_read[NBLK - 2]))
            bank_read[bank] = (sparse["q"],)
            yield

    b_tok_read = {}

    def all_scan_work():
        yield from make_z()
        yield from make_sparse()
        yield from make_queries()

    scan_work = all_scan_work()
    steps(scan_work)

    def heads(ap, width=SSM_P):
        return ap.rearrange("p (h w) -> p h w", w=width)

    def per_head(ap, width=SSM_P):
        n = ap.shape[1]
        return ap.unsqueeze(2).broadcast_to([P, n, width])

    in_turn[:] = [0, 6]
    def finish(c, y, y_ready, a):
        r = dve.do(V.reciprocal, grec, gsum, after=(a,))
        for g in range(SSM_G):
            d = dve.do(V.tensor_scalar, y[:, g * 256:(g + 1) * 256], y[:, g * 256:(g + 1) * 256],
                       grec[:, g:g + 1], None, ALU.mult, after=(r, y_ready))
        turned = []
        for half in range(2):
            bank, ps = next_banks()
            pe.after(*bank_read[bank])
            for j in range(4):
                t = pe.do(T.transpose, ps[:, j * P:(j + 1) * P],
                          y[:, (4 * half + j) * P:(4 * half + j + 1) * P], ident, after=(d,))
            turned.append((bank, ps))
        for half, (bank, ps) in enumerate(turned):
            gain_b = param("ssm_norm", 4 * half, 4).unsqueeze(2).broadcast_to([P, 4, P])
            i, s = side.next()
            dve.after(*scratch_read[i])
            s3 = heads(s[:, 0:512], P)
            m = dve.do(V.tensor_tensor, s3, heads(ps, P), gain_b, ALU.mult, after=(t,))
            bank_read[bank] = (m,)
            done = split_acts(ssm_hi[:, c, 4 * half:4 * half + 4, :],
                              ssm_lo[:, c, 4 * half:4 * half + 4, :], s3, (m, t))
            scratch_read[i] = done
        return (*done, t)

    unfinished = None
    ch_read, xdt_read, small_read = (), (), ()
    st_ready = None
    for c in range(NBLK):
        tokens = slice(c * BLK, (c + 1) * BLK)
        bank, ps = next_banks()
        pe.after(*bank_read[bank])
        t = pe.do(T.matmul, ps[:, 0:16], const("upto"), dta[:, c, :], start=True, stop=True)
        ea_ready = act.do(S.activation, e_acum, ps[:, 0:16], ACT.Exp, after=(t, *ch_read))
        bank_read[bank] = (ea_ready,)
        dx = dve.do(V.tensor_tensor, heads(x_dt), heads(x_tok[:, c, :]), per_head(dt_t[:, c, :]), ALU.mult,
                    after=(*xdt_read,))
        if c < NBLK - 1:
            bank, ps = next_banks()
            pe.after(*bank_read[bank])
            t = pe.do(T.matmul, ps[:, 0:16], const("later"), dta[:, c, :], start=True, stop=True)
            end_ready = act.do(S.activation, to_end, ps[:, 0:16], ACT.Exp, after=(t, *small_read))
            bank_read[bank] = (end_ready,)
            bank, ps = next_banks()
            pe.after(*bank_read[bank])
            t = pe.do(T.matmul, ps[:, 0:16], mean_ones, dta[:, c, :], start=True, stop=True)
            last_ready = act.do(S.activation, e_last, ps[:, 0:16], ACT.Exp, scale=float(D),
                                after=(t, *small_read))
            bank_read[bank] = (last_ready,)
        pe.after(*bank_read[6], *bank_read[7])
        ps_y = bank_cols(6, 2)
        pre = {}

        def decay(g):
            i, w = scratch.next()
            dve.after(*scratch_read[i])
            cb = w[:, 512:512 + P]
            w = w[:, 0:512]
            d = dve.do(V.tensor_tensor, heads(w, P),
                       const("upto").unsqueeze(1).broadcast_to([P, 4, P]),
                       per_head(dta[:, c, 4 * g:4 * g + 4], P), ALU.mult)
            bank, ps = next_banks()
            pe.after(*bank_read[bank])
            t = pe.do(T.matmul, ps, const("later"), w, start=True, stop=True, after=(d,))
            a = act.do(S.activation, w, ps, ACT.Exp, after=(t,))
            bank_read[bank] = (a,)
            pre[g] = (i, w, cb, a)

        def weigh(g):
            i, w, cb, a = pre[g]
            bank, ps = next_banks()
            pe.after(*bank_read[bank])
            t = pe.do(T.matmul, ps[:, 0:P], bT[:, g, tokens], cT[:, g, tokens], start=True, stop=True)
            d = dve.do(V.tensor_tensor, cb, ps[:, 0:P], const("upto"), ALU.mult, after=(t,))
            bank_read[bank] = (d,)
            d = dve.do(V.tensor_tensor, heads(w, P), heads(w, P),
                       cb.unsqueeze(1).broadcast_to([P, 4, P]), ALU.mult, after=(a, d))
            pre[g] = (i, w, d)

        for g in range(3):
            decay(g)
        weigh(0)
        for g in range(SSM_G):
            if g + 1 < SSM_G:
                weigh(g + 1)
            if g == 1 and c > 0:
                finish(*unfinished)
            if c == 0 and g % 2 == 0 or g == 1:
                steps(scan_work)
            i, w, ready = pre[g]
            pe.after(ready, dx)
            for h in range(4):
                col = (4 * g + h) * SSM_P
                t_y = pe.do(T.matmul, ps_y[:, col:col + SSM_P], w[:, h * P:(h + 1) * P],
                            x_dt[:, col:col + SSM_P], start=True, stop=True)
            scratch_read[i] = (t_y,)
            if g == 0:
                decay(3)
        y = z_tok[:, c, :]
        ch_ready = []
        if c > 0:
            for half in range(2):
                bank, ps = next_banks()
                pe.after(*bank_read[bank])
                for g2 in range(2):
                    g = 2 * half + g2
                    t = pe.do(T.matmul, ps[:, g2 * 256:(g2 + 1) * 256], cT[:, g, tokens], state[:, g, :],
                              start=True, stop=True, after=(st_ready,))
                cols = slice(half * 512, (half + 1) * 512)
                d = dve.do(V.tensor_tensor, heads(ch[:, cols]), heads(ps),
                           per_head(e_acum[:, 8 * half:8 * half + 8]), ALU.mult, after=(t, ea_ready))
                bank_read[bank] = (d,)
                ch_ready.append(d)
            st_read = t
        if c:
            steps(scan_work, 2 if c == NBLK - 1 else 1)
        if c < NBLK - 1:
            xe = dve.do(V.tensor_tensor, heads(x_dt), heads(x_dt), per_head(to_end), ALU.mult,
                        after=(end_ready, dx, t_y))
            for half in range(2):
                bank, ps = next_banks()
                pe.after(*bank_read[bank])
                for g2 in range(2):
                    g = 2 * half + g2
                    t = pe.do(T.matmul, ps[:, g2 * 256:(g2 + 1) * 256], b_tok[:, c, g * P:(g + 1) * P],
                              x_dt[:, g * 256:(g + 1) * 256], start=True, stop=True, after=(xe,))
                st = state[:, 2 * half:2 * half + 2, :].rearrange("p g c -> p (g c)")
                if c == 0:
                    d = dve.do(V.tensor_copy, st, ps, after=(t,))
                else:
                    d = dve.do(V.tensor_tensor, heads(st), heads(st), per_head(e_last[:, 8 * half:8 * half + 8]),
                               ALU.mult, after=(last_ready, st_read))
                    d = dve.do(V.tensor_tensor, st, st, ps, ALU.add, after=(d, t))
                bank_read[bank] = (d,)
            st_ready = d
            small_read = (d,)
            xdt_read = (t,)
            b_tok_read[c] = t
        i0, s0 = scratch.next()
        dve.after(*scratch_read[i0])
        i1, s1 = scratch.next()
        dve.after(*scratch_read[i1])
        for half, s in enumerate((s0, s1)):
            cols = slice(half * 512, (half + 1) * 512)
            s = s[:, 0:512]
            d = dve.do(V.tensor_tensor, heads(s), heads(x_tok[:, c, cols]),
                       per_head(param("ssm_d", 8 * half, 8)), ALU.mult)
            d = dve.do(V.tensor_tensor, s, s, ps_y[:, cols], ALU.add, after=(d, t_y))
            if c > 0:
                d = dve.do(V.tensor_tensor, s, s, ch[:, cols], ALU.add, after=(d, ch_ready[half]))
            d = dve.do(V.tensor_tensor, y[:, cols], y[:, cols], s, ALU.mult, after=(d, z_ready[half]))
        y_ready = d
        bank_read[6] = bank_read[7] = (d,)
        scratch_read[i0] = (d,)
        scratch_read[i1] = (d,)
        ch_read = (d,)
        i, sq = scratch.next()
        act.after(*scratch_read[i])
        a = None
        for g in range(SSM_G):
            a = act.do(S.activation, sq[:, 0:256], y[:, g * 256:(g + 1) * 256], ACT.Square,
                       accum_out=gsum[:, g:g + 1], after=(a, y_ready))
        scratch_read[i] = (a,)
        a = act.do(S.activation, gsum, gsum, ACT.Sqrt, scale=1.0 / 256, bias=param("eps"), after=(a,))
        steps(scan_work)
        unfinished = (c, y, y_ready, a)
    ssm_done = finish(*unfinished)
    in_turn[:] = [0, 8]
    for _ in scan_work:
        pass
    scan_over = (*ssm_done, d, t_y)

    nsa_hi = tiles(place("nsa_hi", 4 * TX, F32R, at=at_a(5)), TX)
    nsa_lo = tiles(place("nsa_lo", 4 * TX, F32R, at=at_a(7)), TX)
    nsa_rows = [mod_row[:, 0:4 * 32], place("scores_selected", 2048, at=at_x(2)),
                place("scores_windowed", 2048, at=at_a(8))]
    dist = place("dist", 512, at=late_at)
    TOTALS = 5
    totals = [place(f"total{i}", TX, at=w) for i, w in enumerate((cond_at, cond_at + 2048, late_at + 2048))]
    totals += [sq_sum[:, 0:TX], rstd[:, 0:TX]]
    c_in = load_const("sparse_tables", dist, "dist", sparse["ready"])
    for e in (pe, dve, act):
        e.after(sparse["q"], c_in, gates_ready, *scan_over, *sparse["ready"])

    in_turn[:] = [0, 7]
    units = []
    for blk in range(NBLK):
        for g in range(NSA_G):
            for branch in range(3):
                u = Unit()
                u.blk, u.g, u.branch = blk, g, branch
                u.first, u.last = branch == 0, branch == 2
                if branch == 0:
                    u.keys = [(0, NCMP, vc[0:NCMP, g * HD:(g + 1) * HD])]
                else:
                    v0 = (branch - 1) * P + g * HD
                    u.keys = [(b * BLK, BLK, nv[:, b, v0:v0 + HD]) for b in range(blk + 1)]
                u.dst = tuple(a_[g * HD:(g + 1) * HD, :, blk * BLK:(blk + 1) * BLK]
                              for a_ in (nsa_hi, nsa_lo))
                u.dst_free = scan_over
                units.append(u)

    def sparse_scores(u):
        on = slice(u.g * HD, (u.g + 1) * HD)
        q = lambda h: nq[on, h, u.blk * BLK:(u.blk + 1) * BLK]
        buf = u.rows
        if u.branch == 0:
            u.s = buf[:, 0:4 * NCMP].rearrange("p (h l) -> p h l", l=NCMP)
            bank, ps = next_banks()
            pe.after(*bank_read[bank])
            for h in range(4):
                t = pe.do(T.matmul, ps[:, h * NCMP:(h + 1) * NCMP], q(h), kc[on, 0:NCMP],
                          start=True, stop=True)
            for h in range(4):
                d = dve.do(V.scalar_tensor_tensor, u.s[:, h, :], cd_t[:, u.blk, :], SLOPES[4 * u.g + h],
                           ps[:, h * NCMP:(h + 1) * NCMP], ALU.mult, ALU.add, after=(t, *u.free))
            bank_read[bank] = (d,)
            u.ready = (d,)
            yield
            return
        L = (u.blk + 1) * BLK
        u.s = buf[:, 0:4 * L].rearrange("p (h l) -> p h l", l=L)
        for h in range(4):
            if h == 2:
                yield
            bank, ps = next_banks()
            pe.after(*bank_read[bank])
            t = pe.do(T.matmul, ps[:, 0:L], q(h), nk[on, u.branch - 1, 0:L], start=True, stop=True)
            d = dve.do(V.scalar_tensor_tensor, u.s[:, h, :], dist[:, TX - L:TX], SLOPES[4 * u.g + h],
                       ps[:, 0:L], ALU.mult, ALU.add, after=(t, *u.free))
            bank_read[bank] = (d,)
        u.ready = (d,)

    def sparse_softmax(u):
        g0 = u.branch * NSA_H + 4 * u.g
        valid = None
        if u.branch == 0:
            valid = cv_t[:, u.blk, :].unsqueeze(1).broadcast_to([P, 4, NCMP])
        return divide(u, gates=gates[:, u.blk, g0:g0 + 4], valid=valid)

    ssm_acts = [(ssm_hi[:, :, k, :], ssm_lo[:, :, k, :], ssm_done) for k in range(KD)]
    sb_acts = acts_of(sb_hi, sb_lo, [sb_done] * 4, 4)

    def merge_branch(n, m, name, acts, total, first, buffers):
        bank_g, ps_g = next_banks()
        pe.after(*bank_read[bank_g])
        tok = product("gate", 8 * n + m, h2, SEG_X, ps_g)
        j, sg = buffers.next()
        act.after(*scratch_read[j])
        a = act.do(S.activation, sg[:, 0:TX], ps_g, ACT.Sigmoid, after=(tok,))
        bank_read[bank_g] = (a,)
        yield
        bank, ps = next_banks()
        pe.after(*bank_read[bank])
        tok = product(name, m, acts, SEG_X, ps)
        dst = total if first is None else sg
        d = dve.do(V.tensor_tensor, dst[:, 0:TX], sg[:, 0:TX], ps, ALU.mult, after=(a, tok))
        bank_read[bank] = (d,)
        if first is not None:
            d = dve.do(V.tensor_tensor, total[:, 0:TX], total[:, 0:TX], sg[:, 0:TX], ALU.add,
                       after=(d, first))
        scratch_read[j] = (d,)
        merged[m] = d
        h_used[0] = tok
        yield

    merged, h_used = {}, [None]

    def merge_early():
        for m in range(TOTALS):
            yield from merge_branch(0, m, "br_ssm", ssm_acts, totals[m], None, side)

    nsa_done = run_units(units, sparse_scores, exponents, sparse_softmax, nsa_rows, work=merge_early(), every=2, pause=6)
    attn_over = (*nsa_done, units[-1].read, units[-2].read)
    in_turn[:] = [0, 8]
    scratch.only(0, 1, 2)

    nsa_acts = acts_of(nsa_hi, nsa_lo, [nsa_done] * 4, 4)
    mix_at = [base + 2048 * i for base in (at_x(2), at_a(8), at_a(4), at_a(6)) for i in range(4)]
    mix = []
    for m in range(KD):
        hi = place(f"mix_hi{m}", TX, F32R, at=mix_at[2 * m])
        lo = place(f"mix_lo{m}", TX, F32R, at=mix_at[2 * m + 1])
        if m < TOTALS:
            total = totals[m]
        else:
            i, total = scratch.next()
            dve.after(*scratch_read[i])
            for _ in merge_branch(0, m, "br_ssm", ssm_acts, total, None, side):
                pass
        for _ in merge_branch(1, m, "br_sb", sb_acts, total, merged[m], side):
            pass
        for _ in merge_branch(2, m, "br_nsa", nsa_acts, total, merged[m], side):
            pass
        mix_done = split_acts(hi, lo, total[:, 0:TX], (merged[m], *attn_over))
        if m >= TOTALS:
            scratch_read[i] = mix_done
        mix.append((hi, lo, mix_done))
    h_used = tok = h_used[0]
    scratch.only(*range(5))

    y2 = tiles(place("y2", KD * TX, at=at_a(0)), TX)
    x2 = tiles(place("x2", KD * TX, at=at_a(2)), TX)
    x_in = load("x_again", x2, dram["x_spill"].rearrange("k p t -> p k t"), after=(x_stored, tok))

    y_done = []
    for m in range(KD):
        bank, ps = next_banks()
        pe.after(*bank_read[bank])
        tok = product("out2", m, mix, SEG_X, ps)
        a = act.do(S.copy, y2[:, m, :], ps, after=(tok, h_used))
        bank_read[bank] = (a,)
        y_done.append(a)
        add_square(m, y2[:, m, :], TX, (a,))

    def add_normed(name, squares):
        r = finish_norm(SEG_X)
        for k in range(KD):
            i, t = scratch.next()
            dve.after(*scratch_read[i])
            d = dve.do(V.scalar_tensor_tensor, t[:, 0:TX], y2[:, k, :], param(name, k), rstd[:, 0:TX],
                       ALU.mult, ALU.mult, after=(r,))
            d = dve.do(V.tensor_tensor, x2[:, k, :], x2[:, k, :], t[:, 0:TX], ALU.add, after=(d, x_in))
            scratch_read[i] = (d,)
            if squares:
                add_square(k, x2[:, k, :], TX, (d,))
        rstd_readers[0] = (d,)
        return d

    x_ready[0] = add_normed("post_mix", True)
    y_free = x_ready[0]
    h2 = plain_norm(lambda k: x2[:, k, :], "pre_ffn", x_ready[0], (h_used,))

    g_hi = tiles(place("g2_hi", G_TILES * TX, F32R, at=x_at), TX)
    g_lo = tiles(place("g2_lo", G_TILES * TX, F32R, at=at_a(4)), TX)

    def down2(part, g_acts):
        for m in range(KD):
            bank, ps = next_banks()
            pe.after(*bank_read[bank])
            name, idx = ("down2", part * 8 + m) if part < 2 else ("down2_end", m)
            tok = product(name, idx, g_acts, SEG_X, ps)
            if part == 0:
                d = act.do(S.copy, y2[:, m, :], ps, after=(tok, y_free))
            else:
                d = dve.do(V.tensor_tensor, y2[:, m, :], y2[:, m, :], ps, ALU.add, after=(tok, y_done[m]))
            bank_read[bank] = (d,)
            y_done[m] = d
            if part == 2:
                add_square(m, y2[:, m, :], TX, (d,))
        return tok

    ffn("up2", 0, h2, SEG_X, g_hi, g_lo, (tok,), "conv_ffn2", "conv_ffn2_b", [2, 1, 0], True,
        ACT.Gelu_apprx_tanh, down2)
    last = add_normed("post_ffn", False)

    act.after(last)
    S.dma_start(out.rearrange("k p t -> p k t"), x2).then_inc(stored, 16)
    act.after((stored, 32))

    assert next_piece[0] == len(plan)
    sp_q = Engine(nc, nc.sync, "sp")
    for i, (name, idx) in enumerate(plan):
        _, kt, n = WEIGHTS[name]
        if i >= NRAW:
            sp_q.after(*raw_read[i - NRAW])
        nc.sync.dma_start(raw[i % NRAW][:, 0:kt * n], dram[name][idx]).then_inc(raw_sem[i % NRAW], 16)


def by_feature(w):
    k, m = w.shape
    return w.reshape(k // P, P, m // P, P).transpose(2, 1, 0, 3).reshape(m // P, P, -1)


def by_rows(w, kt, n):
    k, m = w.shape
    return w.reshape(k // P // kt, kt, P, m // n, n).transpose(3, 0, 2, 1, 4).reshape(-1, P, kt * n)


def column(v):
    return np.ascontiguousarray(v.reshape(-1, P).T)


def head_order(per_tile):
    return np.concatenate([np.arange(h * HD, (h + 1) * HD) for h in per_tile])


Q_ORDER = head_order([8 * (i // 4) + i % 4 + 4 * s for i in range(8) for s in range(2)])
NQ_ORDER = head_order([i + 4 * s for i in range(4) for s in range(2)])


def constants():
    r = np.arange(P)
    c = {
        "ident": np.eye(P), "upto": r[:, None] <= r[None, :], "later": r[:, None] > r[None, :],
        "neg_from": -1.0 * (r[:, None] >= r[None, :]),
        "neg_one": -np.ones((P, P)), "before": r[:, None] < r[None, :],
    }
    pick = np.zeros((P, 2))
    pick[[0, 2], 0] = 1
    pick[[1, 3], 1] = 1
    c["pick"] = pick
    rot = np.zeros((P, P))
    half = HD // 2
    for base in (0, HD):
        for i in range(half):
            rot[base + half + i, base + i] = -1.0
            rot[base + i, base + half + i] = 1.0
    c["rope_rot"] = rot
    n_freq = HD // 4
    inv = np.float32(10000.0) ** (-np.arange(n_freq, dtype=np.float32) / np.float32(n_freq))
    t = np.arange(TX)
    ang = np.concatenate([(t // GRID_W).astype(np.float32)[:, None] * inv,
                          (t % GRID_W).astype(np.float32)[:, None] * inv], axis=-1).T
    c["cos"] = np.tile(np.cos(ang), (4, 1))
    c["sin"] = np.tile(np.sin(ang), (4, 1))
    w = np.zeros((P, 384))
    w[:, 0:128][r[None, :] < r[:, None]] = NEG
    w[:, 256:384][r[None, :] > r[:, None]] = NEG
    c["window"] = w
    d = (r[:, None] + 384) - np.arange(512)[None, :]
    c["dist"] = np.where(d >= 0, -1.0 * d, NEG)
    q = np.arange(TX).reshape(NBLK, P)
    end = np.arange(NCMP) * CMP_STRIDE + CMP_LEN - 1
    dc = q[:, :, None] - end[None, None, :]
    c["cmp_dist"] = np.where(dc >= 0, -1.0 * dc, NEG).transpose(1, 0, 2).reshape(P, -1)
    c["cmp_valid"] = (dc >= 0).transpose(1, 0, 2).reshape(P, -1)
    return np.concatenate([np.asarray(c[n], np.float32) for n, _ in CONST_COLS], axis=1)


def kernel(**inputs):
    from concourse import bacc
    from concourse.bass_utils import run_bass_kernel_spmd

    a = {k: np.asarray(v) for k, v in inputs.items()}
    w = {}
    w["mod"] = np.concatenate([by_rows(a["w_mod"][l], 2, 512) for l in range(2)])
    w["in_ab"] = by_feature(a["w_in_ab"][0])
    w["out_ab"] = by_feature(a["w_out_ab"][0])
    w["up"] = np.concatenate([by_feature(a["w_up"][l]) for l in range(2)])
    def rows(v, part):
        return v[PARTS[part][0] * P:sum(PARTS[part]) * P]

    w["down"] = np.concatenate([by_feature(rows(a["w_down"][l], p)) for l in range(2) for p in range(2)])
    w["down_end"] = np.concatenate([by_feature(rows(a["w_down"][l], 2)) for l in range(2)])
    qkv = a["w_qkv"][0]
    w["qk"] = np.concatenate([by_feature(qkv[:, :1024][:, Q_ORDER]), by_feature(qkv[:, 1024:1280])])
    w["v"] = by_rows(qkv[:, 1280:1536], 4, 256)
    w["o"] = by_feature(a["w_o"][0][Q_ORDER])
    sizes = (1024, 2048, 16, 1536, 512, 768, 24, 3072)
    cuts = [sum(sizes[:i]) for i in range(len(sizes) + 1)]
    z, xbc, dt, sb, nq, nkv, ng, mg = (a["w_in_2"][0][:, cuts[i]:cuts[i + 1]] for i in range(8))
    w["z"] = by_rows(z, 2, 512)
    w["xbc"] = by_feature(xbc)
    w["dtg"] = by_rows(np.concatenate([dt, ng], axis=1), 8, 40)
    w["sbqk"] = by_feature(sb[:, :1024])
    w["sbv"] = by_rows(sb[:, 1024:], 2, 512)
    w["nq"] = by_feature(nq[:, NQ_ORDER])
    w["nk"] = by_feature(np.concatenate([nkv[:, 0:384], nkv[:, 512:640]], axis=1))
    w["nv"] = by_rows(np.concatenate([nkv[:, 384:512], nkv[:, 640:768]], axis=1), 4, 256)
    w["gate"] = by_feature(mg)
    w["br_ssm"] = by_feature(a["w_br_ssm_2"][0])
    w["br_sb"] = by_feature(a["w_br_sb_2"][0])
    w["br_nsa"] = by_feature(a["w_br_nsa_2"][0][NQ_ORDER])
    w["out2"] = by_feature(a["w_out_2"][0])
    w["up2"] = by_feature(a["ffn_w_up_2"][0])
    w["down2"] = np.concatenate([by_feature(rows(a["ffn_w_down_2"][0], p)) for p in range(2)])
    w["down2_end"] = by_feature(rows(a["ffn_w_down_2"][0], 2))

    def same(v):
        return np.broadcast_to(v.reshape(1, -1), (P, v.size))

    cond = np.stack([column(a["c"]), column(a["c_ctx"])], axis=2).reshape(P, 2 * KD)
    p = {
        "cond": cond, "b_mod": column(a["b_mod"]), "norm_mix": column(a["norm_mix"]),
        "norm_ffn": column(a["norm_ffn"]), "conv_a": column(a["conv_a"]), "conv_b": column(a["conv_b"]),
        "conv_b_bias": column(a["conv_b_bias"]), "ln_g": column(a["ln_b_gain"]),
        "ln_b": column(a["ln_b_bias"]), "conv_ffn": column(a["w_conv_ffn"]),
        "final_norm": column(a["final_norm"]), "pre_mix": column(a["pre_mix_norm_2"]),
        "ssm_conv_w": column(a["ssm_conv_w_2"]), "ssm_conv_b": column(a["ssm_conv_b_2"]),
        "ssm_norm": column(a["ssm_norm_2"]), "post_mix": column(a["post_mix_norm_2"]),
        "pre_ffn": column(a["pre_ffn_norm_2"]), "conv_ffn2": column(a["ffn_conv_w_2"]),
        "conv_ffn2_b": column(a["ffn_conv_b_2"]), "post_ffn": column(a["post_ffn_norm_2"]),
        "dt_bias": same(a["ssm_dt_bias_2"]), "a_log": same(a["ssm_a_log_2"]), "ssm_d": same(a["ssm_d_2"]),
        "sinks": same(a["sinks"]), "eps": np.full((P, 1), EPS, np.float32),
    }
    for n, width in PARAM_COLS:
        assert p[n].shape == (P, width), (n, p[n].shape, width)
    arrays = {"params": np.concatenate([p[n] for n, _ in PARAM_COLS], axis=1), "consts": constants()}
    arrays["x"] = np.concatenate([a["x"][0], a["ctx"][0]], axis=0).T.reshape(KD, P, TALL)
    for i, s in enumerate("kv"):
        w1 = a[f"cmp_w1_{s}_2"][0].reshape(CMP_LEN, HD, HD).transpose(1, 0, 2)
        b1 = np.zeros((P, CMP_LEN, P), np.float32)
        b2 = np.zeros((P, P), np.float32)
        for g in range(NSA_G):
            b1[g * HD:(g + 1) * HD, :, g * HD:(g + 1) * HD] = w1
            b2[g * HD:(g + 1) * HD, g * HD:(g + 1) * HD] = a[f"cmp_w2_{s}_2"][0]
        arrays[f"cmp_w1_{i}"] = b1.reshape(P, -1)
        arrays[f"cmp_w2_{i}"] = b2
        arrays[f"cmp_pos_{i}"] = np.concatenate([a[f"cmp_pos_{s}_2"][0].T] * NSA_G, axis=0)
    for n, v in w.items():
        count, kt, cols = WEIGHTS[n]
        assert v.shape == (count, P, kt * cols), (n, v.shape)
        arrays[n] = v
    arrays = {n: np.ascontiguousarray(v) for n, v in arrays.items()}

    plan = []
    for _ in range(2):
        nc = bacc.Bacc("TRN2", target_bir_lowering=False, num_devices=1)
        dram = {n: nc.dram_tensor(f"in_{n}", list(v.shape), F32, kind="ExternalInput").ap()
                for n, v in arrays.items()}
        dram["x_spill"] = nc.dram_tensor("x_spill", [KD, P, TX], F32, kind="Internal").ap()
        out = nc.dram_tensor("out_features", [KD, P, TX], F32, kind="ExternalOutput").ap()
        build(nc, dram, out, plan)
    r = run_bass_kernel_spmd(nc, [{f"in_{n}": v for n, v in arrays.items()}], core_ids=[0])
    y = np.asarray(r.results[0]["out_features"])
    return np.ascontiguousarray(y.reshape(D, TX).T)[None]
```
